# Optimizing a Trainium2 kernel written in Bass

```python
import jax, jax.numpy as jnp
from jax import lax
import numpy as np

D_MODEL = 2048
BATCH = 1
SEQ = 256
DEPTH = 1

HEAD_DIM = 128
N_HEADS_FOX = 8
N_HEADS_DIL = 8
DIL_PATTERNS = ((128, 1), (512, 4), (2048, 16))
Q_BLOCK = 128
D_FF = 5632
CONV_WIDTH = 3
EPS = 1e-6
NEG_INF = -1e30
W_FOX = N_HEADS_FOX * HEAD_DIM
W_DIL = N_HEADS_DIL * HEAD_DIM
IN_SPLITS = (W_FOX, W_FOX, W_FOX, N_HEADS_FOX, W_DIL, W_DIL, W_DIL, D_MODEL, D_MODEL)
IN_COLS = sum(IN_SPLITS)

kernel_name = "hybrid_fox_dilated_convffn"

def rms_norm(x, g):
    xf = x.astype(jnp.float32)
    y = xf * lax.rsqrt(jnp.mean(xf * xf, axis=-1, keepdims=True) + EPS)
    return (y * g.astype(jnp.float32)).astype(x.dtype)

def alibi_slopes(n_heads):
    return jnp.asarray(2.0 ** (-8.0 * np.arange(1, n_heads + 1) / n_heads), dtype=jnp.float32)

def split_heads(a, n_heads):
    b, s, _ = a.shape
    return a.reshape(b, s, n_heads, HEAD_DIM).transpose(0, 2, 1, 3)

def merge_heads(a):
    b, h, s, d = a.shape
    return a.transpose(0, 2, 1, 3).reshape(b, s, h * d)

def fox_attention(q, k, v, log_f):
    b, h, s, d = q.shape
    nb = s // Q_BLOCK
    scale = 1.0 / np.sqrt(d)
    c = jnp.cumsum(log_f, axis=-1)
    qb = q.reshape(b, h, nb, Q_BLOCK, d).transpose(2, 0, 1, 3, 4)
    cb = c.reshape(b, h, nb, Q_BLOCK).transpose(2, 0, 1, 3)
    kpos = jnp.arange(s)

    def block(args):
        n, qn, cn = args
        sc = jnp.einsum('bhqd,bhkd->bhqk', qn, k) * scale
        sc = sc + cn[..., :, None] - c[:, :, None, :]
        qpos = n * Q_BLOCK + jnp.arange(Q_BLOCK)
        sc = jnp.where(kpos[None, :] <= qpos[:, None], sc, NEG_INF)
        p = jax.nn.softmax(sc, axis=-1)
        return jnp.einsum('bhqk,bhkd->bhqd', p, v)

    o = lax.map(block, (jnp.arange(nb), qb, cb))
    return o.transpose(1, 2, 0, 3, 4).reshape(b, h, s, d)

def dilated_pattern(q, k, v, slopes, window, dil):
    b, h, s, d = q.shape
    steps = window // dil
    L = s // dil
    nb = -(-L // steps)
    Lp = nb * steps
    scale = 1.0 / np.sqrt(d)

    def to_sub(a):
        return a.reshape(b, h, L, dil, d).transpose(0, 1, 3, 2, 4)

    qs = jnp.pad(to_sub(q), ((0, 0), (0, 0), (0, 0), (0, Lp - L), (0, 0)))
    qb = qs.reshape(b, h, dil, nb, steps, d)

    def band(a):
        ap = jnp.pad(to_sub(a), ((0, 0), (0, 0), (0, 0), (steps, Lp - L), (0, 0)))
        prev = ap[:, :, :, :Lp].reshape(b, h, dil, nb, steps, d)
        cur = ap[:, :, :, steps:].reshape(b, h, dil, nb, steps, d)
        return jnp.concatenate([prev, cur], axis=4)

    kb, vb = band(k), band(v)
    sc = jnp.einsum('bhrnqd,bhrnkd->bhrnqk', qb, kb) * scale
    i = jnp.arange(steps)[:, None]
    j = jnp.arange(2 * steps)[None, :]
    dist = i + steps - j
    ksub = jnp.arange(nb)[:, None, None] * steps + j[None] - steps
    valid = (dist >= 0) & (dist <= steps) & (ksub >= 0)
    penalty = slopes[None, :, None, None, None, None] * (dil * dist).astype(jnp.float32)
    sc = jnp.where(valid, sc - penalty, NEG_INF)
    m = jnp.max(sc, axis=-1, keepdims=True)
    e = jnp.exp(sc - m)
    den = jnp.sum(e, axis=-1)
    o = jnp.einsum('bhrnqk,bhrnkd->bhrnqd', e, vb) / den[..., None]
    lse = m[..., 0] + jnp.log(den)

    def from_sub(a, tail):
        a = a.reshape((b, h, dil, Lp) + tail)[:, :, :, :L]
        perm = (0, 1, 3, 2) + tuple(range(4, 4 + len(tail)))
        return a.transpose(perm).reshape((b, h, s) + tail)

    return from_sub(o, (d,)), from_sub(lse, ())

def dilated_attention(q, k, v, slopes):
    outs, lses = [], []
    for window, dil in DIL_PATTERNS:
        o, l = dilated_pattern(q, k, v, slopes, window, dil)
        outs.append(o)
        lses.append(l)
    o = jnp.stack(outs, axis=0)
    w = jax.nn.softmax(jnp.stack(lses, axis=0), axis=0)
    return jnp.sum(w[..., None] * o, axis=0)

def qk_norm(a, g):
    af = a.astype(jnp.float32)
    af = af * lax.rsqrt(jnp.mean(af * af, axis=-1, keepdims=True) + EPS)
    return af * g.astype(jnp.float32)[None, :, None, :]

def setup_inputs(seed: int = 0) -> dict:
    key = jax.random.key(seed)
    ks = jax.random.split(key, 20)
    f32 = jnp.float32

    def nrm(k, shape, scale):
        return jax.random.normal(k, shape, f32) * scale

    return {
        "x": jax.random.normal(ks[0], (BATCH, SEQ, D_MODEL), f32),
        "g_attn": 1.0 + nrm(ks[1], (DEPTH, D_MODEL), 0.02),
        "w_in": nrm(ks[2], (DEPTH, D_MODEL, IN_COLS), D_MODEL ** -0.5),
        "b_forget": 3.0 + nrm(ks[3], (DEPTH, N_HEADS_FOX), 0.5),
        "g_q_fox": 1.0 + nrm(ks[4], (DEPTH, N_HEADS_FOX, HEAD_DIM), 0.02),
        "g_k_fox": 1.0 + nrm(ks[5], (DEPTH, N_HEADS_FOX, HEAD_DIM), 0.02),
        "g_q_dil": 1.0 + nrm(ks[6], (DEPTH, N_HEADS_DIL, HEAD_DIM), 0.02),
        "g_k_dil": 1.0 + nrm(ks[7], (DEPTH, N_HEADS_DIL, HEAD_DIM), 0.02),
        "w_br_fox": nrm(ks[8], (DEPTH, W_FOX, D_MODEL), W_FOX ** -0.5),
        "w_br_dil": nrm(ks[9], (DEPTH, W_DIL, D_MODEL), W_DIL ** -0.5),
        "w_out": nrm(ks[10], (DEPTH, D_MODEL, D_MODEL), D_MODEL ** -0.5),
        "g_ffn": 1.0 + nrm(ks[11], (DEPTH, D_MODEL), 0.02),
        "w_up": nrm(ks[12], (DEPTH, D_MODEL, 2 * D_FF), D_MODEL ** -0.5),
        "w_conv": nrm(ks[13], (DEPTH, CONV_WIDTH, 2 * D_FF), CONV_WIDTH ** -0.5),
        "b_conv": nrm(ks[14], (DEPTH, 2 * D_FF), 0.02),
        "w_down": nrm(ks[15], (DEPTH, D_FF, D_MODEL), D_FF ** -0.5),
    }

def reference(x, g_attn, w_in, b_forget, g_q_fox, g_k_fox, g_q_dil, g_k_dil,
              w_br_fox, w_br_dil, w_out, g_ffn, w_up, w_conv, b_conv, w_down):
    b, s, _ = x.shape
    offs = np.cumsum(IN_SPLITS)[:-1].tolist()
    slopes = alibi_slopes(N_HEADS_DIL)
    for l in range(DEPTH):
        h = rms_norm(x, g_attn[l])
        proj = h @ w_in[l]
        qa, ka, va, fa, qb, kb, vb, ga, gb = jnp.split(proj, offs, axis=-1)
        q_a = qk_norm(split_heads(qa, N_HEADS_FOX), g_q_fox[l])
        k_a = qk_norm(split_heads(ka, N_HEADS_FOX), g_k_fox[l])
        v_a = split_heads(va, N_HEADS_FOX).astype(jnp.float32)
        log_f = jax.nn.log_sigmoid((fa + b_forget[l]).astype(jnp.float32)).transpose(0, 2, 1)
        o_a = merge_heads(fox_attention(q_a, k_a, v_a, log_f)).astype(x.dtype)
        q_b = qk_norm(split_heads(qb, N_HEADS_DIL), g_q_dil[l])
        k_b = qk_norm(split_heads(kb, N_HEADS_DIL), g_k_dil[l])
        v_b = split_heads(vb, N_HEADS_DIL).astype(jnp.float32)
        o_b = merge_heads(dilated_attention(q_b, k_b, v_b, slopes)).astype(x.dtype)
        merged = jax.nn.sigmoid(ga) * (o_a @ w_br_fox[l]) + jax.nn.sigmoid(gb) * (o_b @ w_br_dil[l])
        x = x + merged @ w_out[l]
        h = rms_norm(x, g_ffn[l])
        u = h @ w_up[l]
        up = jnp.pad(u, ((0, 0), (CONV_WIDTH - 1, 0), (0, 0)))
        wc = w_conv[l]
        conv = sum(wc[t] * up[:, t:t + s] for t in range(CONV_WIDTH)) + b_conv[l]
        gate, val = jnp.split(conv, 2, axis=-1)
        x = x + (jax.nn.silu(gate) * val) @ w_down[l]
    return x


_drawn_inputs = setup_inputs


def setup_inputs(seed=0):
    import zlib

    import numpy as np

    out = dict(_drawn_inputs(seed))
    spreads = {}
    factors = {'g_attn': 6.108,
     'g_q_fox': 8.0,
     'g_k_fox': 8.0,
     'g_q_dil': 8.0,
     'g_k_dil': 8.0,
     'g_ffn': 3.962,
     'b_conv': 3.969}
    for name, (base, spread) in spreads.items():
        noise = np.random.default_rng([zlib.crc32(name.encode()), seed]).standard_normal(out[name].shape)
        drawn = base * np.exp(spread * noise) if base else spread * noise
        out[name] = __import__('jax').numpy.asarray(drawn.astype(out[name].dtype))
    for name, factor in factors.items():
        out[name] = (out[name] * factor).astype(out[name].dtype)
    return out
```

```python
import numpy as np
from contextlib import ExitStack

import concourse.bass as bass
from concourse import mybir

P = 128
SEQ = 256
RT = SEQ // P
DM = 2048
HD = 128
NHEADS = 16
D_FF = 5632
NB = 512
KU = 2
UNIT = KU * NB
UPR = 8
KT = DM // P
RAW_SLOTS = 4
EPS = 1e-6
NEG = -1e30
GROUPS = 4
GATE0 = 12
BR0 = 20
OUT0 = 24
FF0 = 28
BLOCKS = D_FF // NB
CT = NB // P
FA_COL = 3 * 1024
DIL_COL = FA_COL + 8
GATE_COL = DIL_COL + 3 * 1024

S_ID = 0
S_GATT = S_ID + P
S_GFFN = S_GATT + KT
S_GQK = S_GFFN + KT
S_WC = S_GQK + 32
S_BC = S_WC + 3 * 88
S_BF = S_BC + 88
S_SLOPE = S_BF + 16
S_MHALF = S_SLOPE + 8
S_N = S_MHALF + 8
C_U = 0
C_M = C_U + P
C_MASK = C_M + 2 * P
C_ND = C_MASK + 3 * P
C_CNT = C_ND + 3 * P
C_N = C_CNT + 3 * P


def decoder_layer(nc, x, smalls, consts, w_in, w_fox, w_dil, w_out, w_up, w_down, out):
    f32 = mybir.dt.float32
    f32r = mybir.dt.float32r
    ALU = mybir.AluOpType
    ACT = mybir.ActivationFunctionType
    AX = mybir.AxisListType

    def rows_of(w):
        return w.rearrange("(k p) n -> p k n", p=P)

    x_rows = x.rearrange("b (r p) n -> p (b r) n", p=P)
    out_rows = out.rearrange("b (r p) n -> p (b r) n", p=P)
    w_in_v, w_fox_v, w_dil_v = rows_of(w_in), rows_of(w_fox), rows_of(w_dil)
    w_out_v, w_up_v, w_down_v = rows_of(w_out), rows_of(w_up), rows_of(w_down)

    ctx = ExitStack()
    with ctx:
        def sb(name, shape, dt=f32):
            return ctx.enter_context(nc.sbuf_tensor(name, shape, dt))

        def sem(name):
            return ctx.enter_context(nc.semaphore(name))

        raw = sb("raw", [P, RAW_SLOTS, UNIT])
        w_hi = sb("w_hi", [P, UPR, KU, NB], f32r)
        w_lo = sb("w_lo", [P, UPR, KU, NB], f32r)
        actA = sb("actA", [P, KT, 2 * SEQ], f32r)
        actB = sb("actB", [P, KT, 2 * SEQ], f32r)
        work = sb("work", [P, 8192])
        odd = sb("odd", [P, 3072])
        tmp = sb("tmp", [P, RT, NB])
        prob = sb("prob", [P, 3 * P])
        prob_t = sb("prob_t", [P, 3 * P])
        prep = sb("prep", [P, 3 * P])
        smalls_sb = sb("smalls_sb", [P, S_N])
        consts_sb = sb("consts_sb", [P, C_N])
        wf = sb("wf", [P, KT, 16], f32r)
        st = sb("st", [P, 96])
        acc = ctx.enter_context(nc.psum_tensor("acc", [P, 8, 512], f32))
        bank = [acc[:, i, :] for i in range(8)]

        ident = smalls_sb[:, S_ID:S_ID + P]
        upper = consts_sb[:, C_U:C_U + P]
        after = consts_sb[:, C_M:C_M + 2 * P]
        after_t = consts_sb[:, C_M + P:C_M + 2 * P]
        ones = consts_sb[:, C_M:C_M + P]
        mask = consts_sb[:, C_MASK:C_MASK + 3 * P]
        neg_dist = consts_sb[:, C_ND:C_ND + 3 * P]
        count = consts_sb[:, C_CNT:C_CNT + 3 * P]
        mhalf = smalls_sb[:, S_MHALF:S_MHALF + 8]

        xr = work[:, 4096:8192].rearrange("p (r n) -> p r n", r=RT)
        scratch = work[:, 0:4096].rearrange("p (r n) -> p r n", r=RT)
        ga = work[:, 0:4096].rearrange("p (r n) -> p r n", r=RT)
        gb = work[:, 4096:8192].rearrange("p (r n) -> p r n", r=RT)
        wf_raw = work[:, 3072:3200].rearrange("p (k n) -> p k n", k=KT)
        forget = work[:, 3200:3200 + 5 * 16].rearrange("p (a n) -> p a n", a=5)
        heads = (work, odd)

        def q_of(g):
            return heads[g % 2][:, 0:1024].rearrange("p (j s) -> p j s", j=4)

        def k_of(g):
            return heads[g % 2][:, 1024:2048].rearrange("p (j s) -> p j s", j=4)

        def v_of(g):
            return heads[g % 2][:, 2048:3072].rearrange("p (r n) -> p r n", r=RT)

        upad = work[:, 0:4 * 258].rearrange("p (j s) -> p j s", j=CT)
        conv = work[:, 1032:2056].rearrange("p (j s) -> p j s", j=CT)
        silu = work[:, 2056:3080].rearrange("p (j s) -> p j s", j=CT)
        q_now = tmp[:, 0, 0:SEQ]
        v_now = tmp[:, 0, SEQ:2 * SEQ].rearrange("p (r n) -> p r n", r=RT)
        tmp_j = tmp[:, :, :].rearrange("p r (a s) -> p (r a) s", a=2)
        rstd_row = odd[:, 0:SEQ]
        diag = odd[:, 256:512]
        square = odd[:, 512:1536].rearrange("p (r n) -> p r n", r=RT)

        ss8, ms8, rs8 = st[:, 0:8], st[:, 8:16], st[:, 16:24]
        mx, nmx, den, rden = st[:, 24:26], st[:, 26:28], st[:, 28:30], st[:, 30:32]
        xss, xms, xrs = st[:, 32:34], st[:, 34:36], st[:, 36:38]
        ssp = st[:, 40:48]
        fz, fb, fn, fl, lf = (forget[:, i, :] for i in range(5))
        slope = st[:, 64:65]
        lf_keep = st[:, 48:64]

        x_in = [sem(f"x_in{r}") for r in range(RT)]
        smalls_in, consts_in, wf_in, x_again, out_done = (
            sem("smalls_in"), sem("consts_in"), sem("wf_in"), sem("x_again"), sem("out_done"))
        w_loaded = [sem(f"w_loaded{s}") for s in range(RAW_SLOTS)]
        hi_done, lo_done, used = sem("hi_done"), sem("lo_done"), sem("unit_used")
        sums_a, ms_x, rs_x, x_scaled = sem("sums_a"), sem("ms_x"), sem("rs_x"), sem("x_scaled")
        xt_ready, h_hi, h_lo = sem("xt_ready"), sem("h_hi"), sem("h_lo")
        sq_ready, ms_ready, rs_ready, qn_done = sem("sq_ready"), sem("ms_ready"), sem("rs_ready"), sem("qn_done")
        qkt_ready, qkt_done, act_evac = sem("qkt_ready"), sem("qkt_done"), sem("act_evac")
        wf_split, fa_ready, fa_low, fa_arg, fa_exp, fa_ln, lf_ready = (
            sem("wf_split"), sem("fa_ready"), sem("fa_low"), sem("fa_arg"), sem("fa_exp"), sem("fa_ln"),
            sem("lf_ready"))
        prep_ready, scores, maxed, exped, normed = (
            sem("prep_ready"), sem("scores"), sem("maxed"), sem("exped"), sem("normed"))
        pt_ready, pt_copied, o_ready, o_hi, o_lo = (
            sem("pt_ready"), sem("pt_copied"), sem("o_ready"), sem("o_hi"), sem("o_lo"))
        fox_merged, merged, mt_ready, mt_hi, mt_lo = (
            sem("fox_merged"), sem("merged"), sem("mt_ready"), sem("mt_hi"), sem("mt_lo"))
        x2_done, x2_sq, x2t_ready, x2t_hi, x2t_lo = (
            sem("x2_done"), sem("x2_sq"), sem("x2t_ready"), sem("x2t_hi"), sem("x2t_lo"))
        ms2, rs2, diag_ready, bc_ready, bc_done, pad_zero = (
            sem("ms2"), sem("rs2"), sem("diag_ready"), sem("bc_ready"), sem("bc_done"), sem("pad_zero"))
        low_copied, up_added, u_ready, tap2, conv_done, silu_done = (
            sem("low_copied"), sem("up_added"), sem("u_ready"), sem("tap2"), sem("conv_done"), sem("silu_done"))
        a_ready, a_hi, a_lo, d_added = sem("a_ready"), sem("a_hi"), sem("a_lo"), sem("d_added")
        row_max, den_ready, rden_ready, dil_merged, tap1, ss_ready, fa_sum, fa_neg = (
            sem("row_max"), sem("den_ready"), sem("rden_ready"), sem("dil_merged"), sem("tap1"),
            sem("ss_ready"), sem("fa_sum"), sem("fa_neg"))
        biased, slope_now, v_staged = sem("biased"), sem("slope_now"), sem("v_staged")
        block = ctx.enter_context(nc.Block())

        @block.sync
        def _(sp):
            def load(R, u, src):
                n = UPR * R + u
                if not (isinstance(R, int) and n < RAW_SLOTS):
                    sp.wait_ge(lo_done, n - (RAW_SLOTS - 1))
                s = u % RAW_SLOTS
                sp.dma_start(raw[:, s, :].rearrange("p (k n) -> p k n", k=KU), src).then_inc(w_loaded[s], 16)

            def round_of(R, w, col):
                for u in range(UPR):
                    load(R, u, w[:, KU * u:KU * u + KU, bass.ds(col, NB)])

            def down_round(R, blk):
                for u in range(UPR):
                    load(R, u, w_down_v[:, bass.ds(CT * blk + KU * (u % 2), KU), (u // 2) * NB:(u // 2 + 1) * NB])

            sp.dma_start(xr[:, 0, :], x_rows[:, 0, :]).then_inc(x_in[0], 16)
            sp.dma_start(xr[:, 1, :], x_rows[:, 1, :]).then_inc(x_in[1], 16)
            sp.dma_start(smalls_sb[:, :], smalls).then_inc(smalls_in, 16)
            for g in range(GROUPS):
                base = (0 if g < 2 else DIL_COL) + (g % 2) * NB
                for m in range(3):
                    round_of(3 * g + m, w_in_v, base + 1024 * m)
            with sp.Fori(0, 4) as c:
                round_of(GATE0 + 2 * c, w_in_v, GATE_COL + NB * c)
                round_of(GATE0 + 1 + 2 * c, w_in_v, GATE_COL + DM + NB * c)
            with sp.Fori(0, 4) as c:
                for u in range(UPR):
                    w = w_fox_v if u < 4 else w_dil_v
                    load(BR0 + c, u, w[:, KU * (u % 4):KU * (u % 4) + KU, bass.ds(NB * c, NB)])
            with sp.Fori(0, 4) as c:
                round_of(OUT0 + c, w_out_v, NB * c)
            round_of(FF0, w_up_v, 0)
            with sp.Fori(0, BLOCKS - 1) as i:
                round_of(FF0 + 1 + 3 * i, w_up_v, D_FF + NB * i)
                round_of(FF0 + 2 + 3 * i, w_up_v, NB + NB * i)
                down_round(FF0 + 3 + 3 * i, i)
            last = BLOCKS - 1
            round_of(FF0 + 1 + 3 * last, w_up_v, D_FF + NB * last)
            down_round(FF0 + 2 + 3 * last, last)
            for c in range(4):
                for r in range(RT):
                    sp.wait_ge(d_added, 1 + 8 * last + 2 * c + r + 1)
                    sp.dma_start(out_rows[:, r, c * NB:(c + 1) * NB], xr[:, r, c * NB:(c + 1) * NB])\
                        .then_inc(out_done, 16)
            sp.wait_ge(out_done, 16 * 4 * RT)

        @block.tensor
        def _(pe):
            def rows_unit(R, u, act, kts, banks, first, last):
                pe.wait_ge(lo_done, UPR * R + u + 1)
                for r in range(RT):
                    for k, kt in enumerate(kts):
                        a_h = act[:, kt, r * P:(r + 1) * P]
                        a_l = act[:, kt, SEQ + r * P:SEQ + (r + 1) * P]
                        o = banks[r][:, :]
                        nc.tensor.matmul(o, lhsT=a_h, rhs=w_hi[:, u, k, :], start=first and k == 0, stop=False)
                        nc.tensor.matmul(o, lhsT=a_h, rhs=w_lo[:, u, k, :], start=False, stop=False)
                        mm = nc.tensor.matmul(o, lhsT=a_l, rhs=w_hi[:, u, k, :], start=False,
                                              stop=last and k == KU - 1)
                mm.then_inc(used, 1)

            def cols_unit(R, u, banks):
                pe.wait_ge(lo_done, UPR * R + u + 1)
                for k in range(KU):
                    kt = KU * u + k
                    for j in range(CT):
                        hi_w, lo_w = w_hi[:, u, k, j * P:(j + 1) * P], w_lo[:, u, k, j * P:(j + 1) * P]
                        if kt == 0:
                            nc.tensor.matmul(banks[j][:, :], lhsT=hi_w, rhs=actB[:, kt, :], start=True, stop=False)
                        mm = nc.tensor.matmul(banks[j][:, SEQ:], lhsT=lo_w, rhs=actB[:, kt, 0:SEQ],
                                              start=False, stop=False)
                        if kt > 0:
                            mm = nc.tensor.matmul(banks[j][:, :], lhsT=hi_w, rhs=actB[:, kt, :], start=False,
                                                  stop=kt == KT - 1)
                mm.then_inc(used, 1)

            def transpose_block(src, banks, ready):
                for b in range(2):
                    for j in range(2):
                        for r in range(RT):
                            t = nc.tensor.transpose(banks[b][:, j * SEQ + r * P:j * SEQ + (r + 1) * P],
                                                    src(r, (2 * b + j) * P), ident)
                    t.then_inc(ready, 1)

            def transpose_heads(nth, half):
                pe.wait_ge(qn_done, nth + 1)
                if nth or half:
                    pe.wait_ge(qkt_done, 2 * nth + half)
                for j in range(2):
                    for r in range(RT):
                        col = (2 * half + j) * P
                        t = nc.tensor.transpose(bank[7][:, j * SEQ + r * P:j * SEQ + (r + 1) * P],
                                                tmp[:, r, col:col + P], ident)
                t.then_inc(qkt_ready, 1)

            def attend_scores(h, q, k, fox):
                s = bank[4]
                pe.wait_ge(prep_ready, h + 1)
                nc.tensor.matmul(s[:, 0:P], lhsT=q[:, 0:P], rhs=k(0, P), start=True, stop=not fox)
                if fox:
                    nc.tensor.matmul(s[:, 0:P], lhsT=prep[:, 0:P], rhs=after_t, start=False, stop=True)
                mm = nc.tensor.matmul(s[:, P:3 * P], lhsT=q[:, P:2 * P], rhs=k(0, SEQ), start=True, stop=not fox)
                if fox:
                    nc.tensor.matmul(s[:, P:2 * P], lhsT=prep[:, 2 * P:3 * P], rhs=after_t, start=False, stop=False)
                    mm = nc.tensor.matmul(s[:, P:3 * P], lhsT=prep[:, P:2 * P], rhs=after, start=False, stop=True)
                mm.then_inc(scores, 1)

            def attend_transpose(h):
                pe.wait_ge(normed, h + 1)
                for i in range(3):
                    t = nc.tensor.transpose(bank[5][:, i * P:(i + 1) * P], prob[:, i * P:(i + 1) * P], ident)
                t.then_inc(pt_ready, 1)

            def attend_values(h, v0, v1):
                pe.wait_ge(pt_copied, h + 1)
                if not (isinstance(h, int) and h == 0):
                    pe.wait_ge(o_lo, h)
                nc.tensor.matmul(bank[6][:, 0:SEQ], lhsT=v0, rhs=prob_t[:, 0:2 * P], start=True, stop=False)
                nc.tensor.matmul(bank[6][:, P:SEQ], lhsT=v1, rhs=prob_t[:, 2 * P:3 * P],
                                 start=False, stop=True).then_inc(o_ready, 1)

            pe.wait_ge(smalls_in, 16)
            pe.wait_ge(x_scaled, RT)
            for b in range(8):
                for i in range(2):
                    for r in range(RT):
                        kt = 2 * b + i
                        t = nc.tensor.transpose(bank[7 - b][:, i * SEQ + r * P:i * SEQ + (r + 1) * P],
                                                xr[:, r, kt * P:(kt + 1) * P], ident)
                t.then_inc(xt_ready, 1)
            pe.wait_ge(h_lo, KT)

            turned = {12: (0, 0), 14: (0, 1), 20: (1, 0), 22: (1, 1)}
            for g in range(GROUPS):
                for m in range(3):
                    R = 3 * g + m
                    banks = bank[2 * (R % 2):2 * (R % 2) + 2]
                    if R >= 2:
                        before = R - 2
                        if before % 3 == 2:
                            pe.wait_ge(act_evac, before // 3 + 1)
                        else:
                            pe.wait_ge(qn_done, 2 * (before // 3) + before % 3 + 1)
                    for u in range(UPR):
                        rows_unit(R, u, actA, (KU * u, KU * u + 1), banks, u == 0, u == UPR - 1)
                        slot = UPR * m + u
                        j, at = slot // 6, slot % 6
                        h = 4 * (g - 1) + j
                        if g > 0 and at == 1:
                            if j == 0:
                                pe.wait_ge(qkt_done, 4 * g)
                                pe.wait_ge(act_evac, g)
                                pe.wait_ge(consts_in, 16)
                            attend_scores(h, q_of(g - 1)[:, j, :], lambda a, b: k_of(g - 1)[:, j, a:b], g <= 2)
                        elif g > 0 and at == 3:
                            attend_transpose(h)
                        elif g > 0 and at == 5:
                            v = v_of(g - 1)
                            attend_values(h, v[:, 0, j * P:(j + 1) * P], v[:, 1, j * P:(j + 1) * P])
                        if slot in turned:
                            transpose_heads(2 * g + turned[slot][0], turned[slot][1])
                        if g == 0 and slot == 18:
                            pe.wait_ge(wf_split, 2)
                            for r in range(RT):
                                both, low = bank[6][:, 16 * r:16 * r + 16], bank[6][:, 16 * r + 8:16 * r + 16]
                                for kt in range(KT):
                                    a_h = actA[:, kt, r * P:(r + 1) * P]
                                    a_l = actA[:, kt, SEQ + r * P:SEQ + (r + 1) * P]
                                    if kt == 0:
                                        nc.tensor.matmul(both, lhsT=a_h, rhs=wf[:, kt, :], start=True, stop=False)
                                    nc.tensor.matmul(low, lhsT=a_l, rhs=wf[:, kt, 0:8], start=False, stop=False)
                                    if kt > 0:
                                        mm = nc.tensor.matmul(both, lhsT=a_h, rhs=wf[:, kt, :], start=False,
                                                              stop=kt == KT - 1)
                            mm.then_inc(fa_ready, 1)

            pe.wait_ge(qn_done, 2 * GROUPS)
            with pe.Fori(0, 4) as c:
                for m in range(2):
                    R = GATE0 + m + 2 * c
                    pe.wait_ge(act_evac, 3 + m + 2 * c)
                    for u in range(UPR):
                        rows_unit(R, u, actA, (KU * u, KU * u + 1), bank[2 * m:2 * m + 2], u == 0, u == UPR - 1)
                        if m == 0 and u == 1:
                            attend_scores(12 + c, q_now, lambda a, b: odd[:, bass.ds(1024 + SEQ * c + a, b - a)], False)
                        elif m == 0 and u == 4:
                            attend_transpose(12 + c)
                        elif m == 0 and u == 7:
                            attend_values(12 + c, v_now[:, 0, :], v_now[:, 1, :])

            def branch_round(c):
                pe.wait_ge(act_evac, 4 + 7)
                for u in range(UPR):
                    pair = bank[0:2] if u < 4 else bank[2:4]
                    rows_unit(BR0 + c, u, actB, (KU * u, KU * u + 1), pair, u % 4 == 0, u % 4 == 3)
                    yield u

            pe.wait_ge(o_lo, NHEADS)
            for u in branch_round(0):
                if u == 3:
                    pe.wait_ge(act_evac, 4 + 8)
            with pe.Fori(1, 4) as c:
                pe.wait_ge(fox_merged, c)
                for u in branch_round(c):
                    if u == 2:
                        pe.wait_ge(merged, c)
                        transpose_block(lambda r, col: tmp[:, r, col:col + P], bank[4:6], mt_ready)

            for c in range(4):
                R, banks = OUT0 + c, bank[2 * (c % 2):2 * (c % 2) + 2]
                if c == 0:
                    pe.wait_ge(fox_merged, 4)
                    pe.wait_ge(mt_lo, 6)
                elif c == 1:
                    pe.wait_ge(merged, 4)
                else:
                    pe.wait_ge(x2_done, c - 1)
                for u in range(UPR):
                    if c == 0 and u == 6:
                        pe.wait_ge(mt_lo, 8)
                    rows_unit(R, u, actA, (KU * u, KU * u + 1), banks, u == 0, u == UPR - 1)
                    if u == 2 and c == 0:
                        pe.wait_ge(merged, 4)
                        transpose_block(lambda r, col: tmp[:, r, col:col + P], bank[4:6], mt_ready)
                    elif u == 2:
                        pe.wait_ge(x2_done, c)
                        if c > 1:
                            pe.wait_ge(x2t_lo, 4 * (c - 1))
                        transpose_block(lambda r, col: xr[:, r, (c - 1) * NB + col:(c - 1) * NB + col + P],
                                        bank[4:6], x2t_ready)

            pe.wait_ge(x2t_lo, 12)
            for u in range(UPR):
                if u == 6:
                    pe.wait_ge(x2t_lo, 16)
                cols_unit(FF0, u, bank[4:8])
                if u == 2:
                    pe.wait_ge(x2_done, 4)
                    transpose_block(lambda r, col: xr[:, r, 3 * NB + col:3 * NB + col + P], bank[0:2], x2t_ready)
                if u == 5:
                    pe.wait_ge(diag_ready, 1)
                    nc.tensor.matmul(bank[2][:, 0:SEQ], lhsT=ones, rhs=diag, start=True, stop=True)\
                        .then_inc(bc_ready, 1)
            pe.wait_ge(bc_done, 1)

            def up_round(R, banks):
                for u in range(UPR):
                    cols_unit(R, u, banks)

            def down_round(R, i, last):
                pe.wait_ge(a_lo, i + 1)
                pe.wait_ge(up_added, 2 * i + 2)
                for u in range(UPR):
                    if u == 4 and not last:
                        pe.wait_ge(up_added, 2 * i + 3)
                    if u == 6:
                        pe.wait_ge(d_added, 1 + 8 * i + 4)
                    c = u // 2
                    rows_unit(R, u, actA, (KU * (u % 2), KU * (u % 2) + 1), bank[2 * c:2 * c + 2],
                              u % 2 == 0, u % 2 == 1)

            with pe.Fori(0, BLOCKS - 1) as i:
                up_round(FF0 + 1 + 3 * i, bank[0:4])
                pe.wait_ge(d_added, 1 + 8 * i)
                up_round(FF0 + 2 + 3 * i, bank[4:8])
                down_round(FF0 + 3 + 3 * i, i, False)
            up_round(FF0 + 1 + 3 * (BLOCKS - 1), bank[0:4])
            pe.wait_ge(d_added, 1 + 8 * (BLOCKS - 1))
            down_round(FF0 + 2 + 3 * (BLOCKS - 1), BLOCKS - 1, True)

        @block.scalar
        def _(act):
            def high(R, u):
                act.wait_ge(w_loaded[u % RAW_SLOTS], 16 * (2 * R + u // RAW_SLOTS + 1))
                if not (isinstance(R, int) and R == 0):
                    act.wait_ge(used, UPR * (R - 1) + u + 1)
                nc.scalar.activation(w_hi[:, u, :, :], raw[:, u % RAW_SLOTS, :].rearrange("p (k n) -> p k n", k=KU),
                                     ACT.Copy).then_inc(hi_done, 1)

            def exps(h):
                act.wait_ge(maxed, h + 1)
                nc.scalar.activation(prob[:, 0:P], prob[:, 0:P], ACT.Exp, bias=nmx[:, 0:1],
                                     accum_out=den[:, 0:1])
                nc.scalar.activation(prob[:, P:3 * P], prob[:, P:3 * P], ACT.Exp, bias=nmx[:, 1:2],
                                     accum_out=den[:, 1:2]).then_inc(exped, 1)

            def copy_pt(h):
                act.wait_ge(pt_ready, h + 1)
                nc.scalar.activation(prob_t[:, :], bank[5][:, 0:3 * P], ACT.Copy).then_inc(pt_copied, 1)

            def out_high(h):
                act.wait_ge(o_ready, h + 1)
                dst = actB[:, h, 0:SEQ] if isinstance(h, int) else actB[:, bass.ds(h, 1), 0:SEQ]
                nc.scalar.activation(dst, bank[6][:, 0:SEQ], ACT.Copy).then_inc(o_hi, 1)

            def merged_high(c):
                for b in range(2):
                    act.wait_ge(mt_ready, 2 * c + b + 1)
                    kt = 4 * c + 2 * b
                    nc.scalar.activation(actA[:, bass.ds(kt, 2), 0:SEQ],
                                         bank[4 + b][:, :].rearrange("p (j s) -> p j s", j=2),
                                         ACT.Copy).then_inc(mt_hi, 1)

            def x2_squares(c):
                act.wait_ge(x2_done, c + 1)
                if c:
                    act.wait_ge(x2_sq, RT * c)
                for r in range(RT):
                    nc.scalar.activation(square[:, r, :], xr[:, r, c * NB:(c + 1) * NB], ACT.Square,
                                         accum_out=ssp[:, 4 * r + c:4 * r + c + 1]).then_inc(x2_sq, 1)

            def x2t_high(c, banks):
                for b in range(2):
                    act.wait_ge(x2t_ready, 2 * c + b + 1)
                    for j in range(2):
                        kt = 4 * c + 2 * b + j
                        nc.scalar.activation(actB[:, kt, 0:SEQ], banks[b][:, j * SEQ:(j + 1) * SEQ], ACT.Copy,
                                             scale=smalls_sb[:, S_GFFN + kt:S_GFFN + kt + 1]).then_inc(x2t_hi, 1)

            act.wait_ge(x_in[0], 16)
            nc.scalar.activation(scratch[:, 0, :], xr[:, 0, :], ACT.Square, accum_out=xss[:, 0:1]).then_inc(sums_a, 1)
            act.wait_ge(rs_x, 1)
            act.dma_start(wf_raw, w_in_v[:, :, FA_COL:FA_COL + 8]).then_inc(wf_in, 16)
            nc.scalar.activation(xr[:, 1, :], xr[:, 1, :], ACT.Copy, scale=xrs[:, 1:2]).then_inc(x_scaled, 1)
            act.wait_ge(smalls_in, 16)
            for b in range(8):
                if b < 2:
                    high(0, b)
                act.wait_ge(xt_ready, b + 1)
                for i in range(2):
                    kt = 2 * b + i
                    nc.scalar.activation(actA[:, kt, 0:SEQ], bank[7 - b][:, i * SEQ:(i + 1) * SEQ], ACT.Copy,
                                         scale=smalls_sb[:, S_GATT + kt:S_GATT + kt + 1]).then_inc(h_hi, 1)
                if b in (3, 5):
                    high(0, b // 2 + 1)
            for u in range(4, UPR):
                high(0, u)

            turned = {12: (0, 0), 14: (0, 1), 20: (1, 0), 22: (1, 1)}
            for g in range(GROUPS):
                for m in range(3):
                    R = 3 * g + m
                    pair = 2 * (R % 2)
                    for u in range(UPR):
                        high(R + 1, u)
                        slot = UPR * m + u
                        j, at = slot // 6, slot % 6
                        h = 4 * (g - 1) + j
                        if g > 0 and at == 1:
                            exps(h)
                        elif g > 0 and at == 3:
                            copy_pt(h)
                        elif g > 0 and at == 5:
                            out_high(h)
                        if slot in turned:
                            nth = 2 * g + turned[slot][0]
                            act.wait_ge(qkt_ready, 2 * nth + turned[slot][1] + 1)
                            dst = (q_of(g), k_of(g))[turned[slot][0]]
                            for jj in range(2):
                                head = 2 * turned[slot][1] + jj
                                col = S_GQK + 4 * nth + head
                                t = nc.scalar.activation(dst[:, head, :], bank[7][:, jj * SEQ:(jj + 1) * SEQ],
                                                         ACT.Copy, scale=smalls_sb[:, col:col + 1])
                            t.then_inc(qkt_done, 1)
                        if u == UPR - 1:
                            act.wait_ge(used, UPR * R + UPR)
                            if m < 2:
                                if R:
                                    act.wait_ge(qkt_ready, 2 * (2 * g + m))
                                for r in range(RT):
                                    t = nc.scalar.activation(tmp[:, r, :], bank[pair + r][:, :], ACT.Square)
                                t.then_inc(sq_ready, 1)
                            else:
                                for r in range(RT):
                                    t = nc.scalar.activation(v_of(g)[:, r, :], bank[pair + r][:, :], ACT.Copy)
                                t.then_inc(act_evac, 1)
                        if g == 0 and slot == 6:
                            act.wait_ge(wf_in, 16)
                            nc.scalar.activation(wf[:, :, 0:8], wf_raw, ACT.Copy).then_inc(wf_split, 1)
                        if g == 0 and slot == 8:
                            act.dma_start(consts_sb[:, :], consts).then_inc(consts_in, 16)
                        if g == 0 and slot == 19:
                            act.wait_ge(fa_ready, 1)
                            low = bank[6][:, 0:32].rearrange("p (r c n) -> p r c n", r=RT, c=2)[:, :, 1, :]
                            nc.scalar.activation(fl.rearrange("p (r n) -> p r n", r=RT), low, ACT.Copy)\
                                .then_inc(fa_low, 1)
                        if g == 0 and slot == 20:
                            act.wait_ge(fa_arg, 1)
                            nc.scalar.activation(fn, fn, ACT.Exp).then_inc(fa_exp, 1)
                            act.wait_ge(fa_exp, 1)
                            nc.scalar.activation(fn, fn, ACT.Ln, bias=1.0).then_inc(fa_ln, 1)

            with act.Fori(0, 4) as c:
                for m in range(2):
                    R = GATE0 + m + 2 * c
                    for u in range(UPR):
                        high(R + 1, u)
                        if m == 0 and u == 1:
                            exps(12 + c)
                        elif m == 0 and u == 4:
                            copy_pt(12 + c)
                        elif m == 0 and u == 7:
                            out_high(12 + c)
                        if u == UPR - 1:
                            act.wait_ge(used, UPR * R + UPR)
                            for r in range(RT):
                                t = nc.scalar.activation((ga, gb)[m][:, r, bass.ds(c * NB, NB)],
                                                         bank[2 * m + r][:, :], ACT.Sigmoid)
                            t.then_inc(act_evac, 1)

            for u in range(UPR):
                high(BR0 + 1, u)
            with act.Fori(1, 4) as c:
                for u in range(UPR):
                    high(BR0 + 1 + c, u)
                    if u == 2:
                        merged_high(c - 1)

            for c in range(4):
                R = OUT0 + c
                for u in range(UPR):
                    high(R + 1, u)
                    if u == 1 and c == 0:
                        act.wait_ge(merged, 4)
                        act.dma_start(xr[:, :, :], x_rows).then_inc(x_again, 16)
                    if u == 2 and c == 0:
                        merged_high(3)
                    elif u == 2:
                        x2t_high(c - 1, bank[4:6])
                x2_squares(c)

            def low_copy(R, q, b0, first=False):
                act.wait_ge(used, UPR * R + UPR)
                nc.scalar.activation(tmp_j, acc[:, b0:b0 + CT, SEQ:2 * SEQ], ACT.Copy).then_inc(low_copied, 1)

            def newest_tap(q, ct):
                act.wait_ge(u_ready, q + 1)
                for j in range(CT):
                    t = nc.scalar.activation(conv[:, j, :], upad[:, j, 2:2 + SEQ], ACT.Identity,
                                             scale=smalls_sb[:, bass.ds(S_WC + 2 * 88 + ct + j, 1)],
                                             bias=smalls_sb[:, bass.ds(S_BC + ct + j, 1)])
                t.then_inc(tap2, 1)

            def gate_silu(q, i):
                act.wait_ge(conv_done, q + 1)
                nc.scalar.activation(silu, conv, ACT.Silu).then_inc(silu_done, 1)

            def hidden_high(i):
                act.wait_ge(a_ready, i + 1)
                nc.scalar.activation(actA[:, 0:CT, 0:SEQ], tmp_j, ACT.Copy).then_inc(a_hi, 1)

            for u in range(UPR):
                high(FF0 + 1, u)
                if u == 2:
                    x2t_high(3, bank[0:2])
                if u == 5:
                    act.wait_ge(bc_ready, 1)
                    nc.scalar.activation(rstd_row, bank[2][:, 0:SEQ], ACT.Copy).then_inc(bc_done, 1)
            low_copy(FF0, 0, 4)

            def ff_block(i, last):
                V = FF0 + 1 + 3 * i
                for u in range(UPR):
                    high(V + 1, u)
                    if u == 0:
                        newest_tap(2 * i, 4 * i)
                    elif u == 2:
                        gate_silu(2 * i, i)
                act.wait_ge(u_ready, 2 * i + 1)
                low_copy(V, 2 * i + 1, 0)
                if last:
                    newest_tap(2 * i + 1, 44 + 4 * i)
                    hidden_high(i)
                    return
                for u in range(UPR):
                    high(V + 2, u)
                    if u == 0:
                        newest_tap(2 * i + 1, 44 + 4 * i)
                    elif u == 3:
                        hidden_high(i)
                act.wait_ge(a_lo, i + 1)
                low_copy(V + 1, 2 * i + 2, 4)
                for u in range(UPR):
                    high(V + 3, u)

            with act.Fori(0, BLOCKS - 1) as i:
                ff_block(i, False)
            ff_block(BLOCKS - 1, True)

        @block.vector
        def _(dve):
            def low(R, u):
                dve.wait_ge(hi_done, UPR * R + u + 1)
                nc.vector.tensor_tensor(w_lo[:, u, :, :],
                                        raw[:, u % RAW_SLOTS, :].rearrange("p (k n) -> p k n", k=KU),
                                        w_hi[:, u, :, :].bitcast(f32), ALU.subtract).then_inc(lo_done, 1)

            def softmax_head(h, bias, dil):
                dve.wait_ge(scores, h + 1)
                parts = ((0, P), (P, 3 * P))
                if dil:
                    nc.vector.tensor_tensor(prob[:, :], bank[4][:, 0:3 * P], bias[:, :], ALU.add).then_inc(biased, 1)
                    dve.wait_ge(biased, h - 7)
                for i, (a, b) in enumerate(parts):
                    if dil:
                        t = nc.vector.reduce_max(mx[:, i:i + 1], prob[:, a:b], AX.X)
                    else:
                        t = nc.vector.tensor_tensor_reduce(out=prob[:, a:b], in0=bank[4][:, a:b], in1=bias[:, a:b],
                                                           scale=1.0, scalar=-3.0e38, op0=ALU.add, op1=ALU.max,
                                                           accum_out=mx[:, i:i + 1])
                t.then_inc(row_max, 1)
                dve.wait_ge(row_max, h + 1)
                nc.vector.tensor_scalar(nmx, mx, -1.0, None, ALU.mult).then_inc(maxed, 1)
                dve.wait_ge(exped, h + 1)
                if dil:
                    for i, (a, b) in enumerate(parts):
                        t = nc.vector.tensor_tensor_reduce(out=prob[:, a:b], in0=prob[:, a:b], in1=count[:, a:b],
                                                           scale=1.0, scalar=0.0, op0=ALU.mult, op1=ALU.add,
                                                           accum_out=den[:, i:i + 1])
                    t.then_inc(den_ready, 1)
                    dve.wait_ge(den_ready, h - 7)
                nc.vector.reciprocal(rden, den).then_inc(rden_ready, 1)
                dve.wait_ge(rden_ready, h + 1)
                for i, (a, b) in enumerate(parts):
                    t = nc.vector.tensor_scalar(prob[:, a:b], prob[:, a:b], rden[:, i:i + 1], None, ALU.mult)
                t.then_inc(normed, 1)

            def out_low(h):
                dve.wait_ge(o_hi, h + 1)
                at = h if isinstance(h, int) else None
                dst = actB[:, h, SEQ:2 * SEQ] if at is not None else actB[:, bass.ds(h, 1), SEQ:2 * SEQ]
                src = actB[:, h, 0:SEQ] if at is not None else actB[:, bass.ds(h, 1), 0:SEQ]
                nc.vector.tensor_tensor(dst, bank[6][:, 0:SEQ], src.bitcast(f32), ALU.subtract).then_inc(o_lo, 1)

            def merged_low(c):
                for b in range(2):
                    dve.wait_ge(mt_hi, 2 * c + b + 1)
                    kt = 4 * c + 2 * b
                    nc.vector.tensor_tensor(actA[:, bass.ds(kt, 2), SEQ:2 * SEQ],
                                            bank[4 + b][:, :].rearrange("p (j s) -> p j s", j=2),
                                            actA[:, bass.ds(kt, 2), 0:SEQ].bitcast(f32),
                                            ALU.subtract).then_inc(mt_lo, 1)

            def scaled_low(dst_src, kt, bank_half, gains, done):
                dst, src = dst_src
                nc.vector.scalar_tensor_tensor(out=dst, in0=bank_half, scalar=smalls_sb[:, gains + kt:gains + kt + 1],
                                               in1=src.bitcast(f32), op0=ALU.mult, op1=ALU.subtract)\
                    .then_inc(done, 1)

            def x2t_low(c, banks):
                for b in range(2):
                    dve.wait_ge(x2t_hi, 4 * c + 2 * b + 2)
                    for j in range(2):
                        kt = 4 * c + 2 * b + j
                        scaled_low((actB[:, kt, SEQ:2 * SEQ], actB[:, kt, 0:SEQ]), kt,
                                   banks[b][:, j * SEQ:(j + 1) * SEQ], S_GFFN, x2t_lo)

            dve.wait_ge(x_in[1], 16)
            nc.vector.tensor_tensor_reduce(out=scratch[:, 1, :], in0=xr[:, 1, :], in1=xr[:, 1, :], scale=1.0,
                                           scalar=0.0, op0=ALU.mult, op1=ALU.add, accum_out=xss[:, 1:2])\
                .then_inc(sums_a, 1)
            dve.wait_ge(sums_a, 2)
            nc.vector.tensor_scalar(xms, xss, 1.0 / DM, EPS, ALU.mult, ALU.add).then_inc(ms_x, 1)
            dve.wait_ge(rs_x, 1)
            nc.vector.tensor_scalar(xr[:, 0, :], xr[:, 0, :], xrs[:, 0:1], None, ALU.mult).then_inc(x_scaled, 1)
            dve.wait_ge(smalls_in, 16)
            for b in range(8):
                if b < 2:
                    low(0, b)
                dve.wait_ge(h_hi, 2 * b + 2)
                for i in range(2):
                    kt = 2 * b + i
                    scaled_low((actA[:, kt, SEQ:2 * SEQ], actA[:, kt, 0:SEQ]), kt,
                               bank[7 - b][:, i * SEQ:(i + 1) * SEQ], S_GATT, h_lo)
                if b in (3, 5):
                    low(0, b // 2 + 1)
            for u in range(4, UPR):
                low(0, u)

            def normalise(nth):
                pair = 2 * ((3 * (nth // 2) + nth % 2) % 2)
                dve.wait_ge(rs_ready, nth + 1)
                for r in range(RT):
                    t = nc.vector.tensor_tensor(
                        tmp[:, r, :].rearrange("p (j d) -> p j d", j=4),
                        bank[pair + r][:, :].rearrange("p (j d) -> p j d", j=4),
                        rs8[:, 4 * r:4 * r + 4].rearrange("p (j a) -> p j a", a=1).broadcast_to([P, 4, HD]), ALU.mult)
                t.then_inc(qn_done, 1)

            for g in range(GROUPS):
                for m in range(3):
                    R = 3 * g + m
                    for u in range(UPR):
                        low(R + 1, u)
                        slot = UPR * m + u
                        j, at = slot // 6, slot % 6
                        h = 4 * (g - 1) + j
                        if u == 0 and m > 0:
                            normalise(2 * g + m - 1)
                        if g > 0 and at == 1:
                            if g == 3:
                                dve.wait_ge(prep_ready, h + 1)
                            softmax_head(h, prep if g == 3 else mask, g == 3)
                        elif g > 0 and at == 5:
                            out_low(h)
                        if u == UPR - 1 and m < 2:
                            dve.wait_ge(sq_ready, 2 * g + m + 1)
                            nc.vector.tensor_reduce(out=ss8, in_=tmp[:, :, :].rearrange("p r (j d) -> p (r j) d", j=4),
                                                    axis=AX.X, op=ALU.add).then_inc(ss_ready, 1)
                            dve.wait_ge(ss_ready, 2 * g + m + 1)
                            if m == 0:
                                t = nc.vector.tensor_scalar(ms8, ss8, HD * EPS, None, ALU.add)
                            else:
                                t = nc.vector.tensor_scalar(ms8, ss8, 1.0 / HD, EPS, ALU.mult, ALU.add)
                            t.then_inc(ms_ready, 1)
                        if g == 0 and slot == 6:
                            dve.wait_ge(wf_split, 1)
                            nc.vector.tensor_tensor(wf[:, :, 8:16], wf_raw, wf[:, :, 0:8].bitcast(f32),
                                                    ALU.subtract).then_inc(wf_split, 1)
                        if g == 0 and slot == 19:
                            dve.wait_ge(fa_low, 1)
                            hi_part = bank[6][:, 0:32].rearrange("p (r c n) -> p r c n", r=RT, c=2)[:, :, 0, :]
                            nc.vector.tensor_tensor(fz.rearrange("p (r n) -> p r n", r=RT), hi_part,
                                                    fl.rearrange("p (r n) -> p r n", r=RT), ALU.add)\
                                .then_inc(fa_sum, 1)
                            dve.wait_ge(fa_sum, 1)
                            nc.vector.tensor_tensor(fz, fz, smalls_sb[:, S_BF:S_BF + 16], ALU.add).then_inc(fa_sum, 1)
                            dve.wait_ge(fa_sum, 2)
                            nc.vector.tensor_scalar(fb, fz, -1.0, None, ALU.mult).then_inc(fa_neg, 1)
                            dve.wait_ge(fa_neg, 1)
                            nc.vector.tensor_tensor(fn, fz, fb, ALU.min).then_inc(fa_arg, 1)
                        if g == 0 and slot == 21:
                            dve.wait_ge(fa_ln, 1)
                            nc.vector.scalar_tensor_tensor(out=lf_keep, in0=fz, scalar=0.0, in1=fn, op0=ALU.min,
                                                           op1=ALU.subtract).then_inc(lf_ready, 1)
                            dve.wait_ge(consts_in, 16)

            with dve.Fori(0, 4) as c:
                for m in range(2):
                    R = GATE0 + m + 2 * c
                    for u in range(UPR):
                        low(R + 1, u)
                        if m == 0 and u == 1:
                            softmax_head(12 + c, prep, True)
                        elif m == 0 and u == 7:
                            out_low(12 + c)

            def fox_part(c):
                dve.wait_ge(used, UPR * (BR0 + c) + 4)
                for r in range(RT):
                    t = nc.vector.tensor_tensor(tmp[:, r, :], bank[r][:, :], ga[:, r, bass.ds(c * NB, NB)], ALU.mult)
                t.then_inc(fox_merged, 1)

            def dil_part(c):
                dve.wait_ge(used, UPR * (BR0 + c) + UPR)
                for r in range(RT):
                    part = gb[:, r, bass.ds(c * NB, NB)]
                    t = nc.vector.tensor_tensor(part, bank[2 + r][:, :], part, ALU.mult)
                t.then_inc(dil_merged, 1)
                dve.wait_ge(dil_merged, c + 1)
                nc.vector.tensor_tensor(tmp[:, :, :], tmp[:, :, :], gb[:, :, bass.ds(c * NB, NB)], ALU.add)\
                    .then_inc(merged, 1)

            dve.wait_ge(act_evac, 4 + 8)
            for u in range(UPR):
                low(BR0 + 1, u)
                if u == 3:
                    fox_part(0)
            dil_part(0)
            with dve.Fori(1, 4) as c:
                for u in range(UPR):
                    low(BR0 + 1 + c, u)
                    if u == 3:
                        merged_low(c - 1)
                        dve.wait_ge(mt_ready, 2 * c)
                        fox_part(c)
                dil_part(c)

            for c in range(4):
                R = OUT0 + c
                for u in range(UPR):
                    low(R + 1, u)
                    if u == 3 and c == 0:
                        merged_low(3)
                    elif u == 3:
                        x2t_low(c - 1, bank[4:6])
                if c == 0:
                    dve.wait_ge(x_again, 16)
                dve.wait_ge(used, UPR * R + UPR)
                for r in range(RT):
                    part = xr[:, r, c * NB:(c + 1) * NB]
                    t = nc.vector.tensor_tensor(part, bank[2 * (c % 2) + r][:, :], part, ALU.add)
                t.then_inc(x2_done, 1)
                if c == 0:
                    nc.vector.memset(upad[:, :, 0:2], 0.0).then_inc(d_added, 1)

            def add_up(q, b0):
                dve.wait_ge(low_copied, q + 1)
                nc.vector.tensor_tensor(tmp_j, acc[:, b0:b0 + CT, 0:SEQ], tmp_j, ALU.add).then_inc(up_added, 1)
                dve.wait_ge(up_added, q + 1)
                nc.vector.tensor_tensor(upad[:, :, 2:2 + SEQ], tmp_j,
                                        rstd_row.rearrange("p (a s) -> p a s", a=1).broadcast_to([P, CT, SEQ]),
                                        ALU.mult).then_inc(u_ready, 1)

            def older_taps(q, ct):
                dve.wait_ge(tap2, q + 1)
                for tap, done in ((1, tap1), (0, conv_done)):
                    for j in range(CT):
                        t = nc.vector.scalar_tensor_tensor(
                            out=conv[:, j, :], in0=upad[:, j, tap:tap + SEQ],
                            scalar=smalls_sb[:, bass.ds(S_WC + 88 * tap + ct + j, 1)], in1=conv[:, j, :],
                            op0=ALU.mult, op1=ALU.add)
                    t.then_inc(done, 1)
                    dve.wait_ge(done, q + 1)

            def hidden(i):
                dve.wait_ge(silu_done, i + 1)
                nc.vector.tensor_tensor(tmp_j, conv, silu, ALU.mult).then_inc(a_ready, 1)

            def hidden_low(i):
                dve.wait_ge(a_hi, i + 1)
                nc.vector.tensor_tensor(actA[:, 0:CT, SEQ:2 * SEQ], tmp_j, actA[:, 0:CT, 0:SEQ].bitcast(f32),
                                        ALU.subtract).then_inc(a_lo, 1)

            def add_down(R, c):
                dve.wait_ge(used, UPR * R + 2 * c + 2)
                for r in range(RT):
                    part = xr[:, r, c * NB:(c + 1) * NB]
                    nc.vector.tensor_tensor(part, bank[2 * c + r][:, :], part, ALU.add).then_inc(d_added, 1)

            for u in range(UPR):
                low(FF0 + 1, u)
                if u == 0:
                    dve.wait_ge(x2_sq, 8)
                    nc.vector.tensor_reduce(out=xss, in_=ssp.rearrange("p (r c) -> p r c", r=RT), axis=AX.X,
                                            op=ALU.add).then_inc(sums_a, 1)
                    dve.wait_ge(sums_a, 3)
                    nc.vector.tensor_scalar(xms, xss, 1.0 / DM, EPS, ALU.mult, ALU.add).then_inc(ms_x, 1)
                elif u == 2:
                    dve.wait_ge(rs_x, 2)
                    for r in range(RT):
                        t = nc.vector.tensor_scalar(diag[:, r * P:(r + 1) * P], ident, xrs[:, r:r + 1], None, ALU.mult)
                    t.then_inc(diag_ready, 1)
                elif u == 3:
                    x2t_low(3, bank[0:2])
            dve.wait_ge(bc_done, 1)
            add_up(0, 4)

            def ff_block(i, last):
                V = FF0 + 1 + 3 * i
                for u in range(UPR):
                    low(V + 1, u)
                    if u == 1:
                        older_taps(2 * i, 4 * i)
                add_up(2 * i + 1, 0)
                if last:
                    older_taps(2 * i + 1, 44 + 4 * i)
                    hidden(i)
                    hidden_low(i)
                    for c in range(4):
                        add_down(V + 1, c)
                    return
                for u in range(UPR):
                    low(V + 2, u)
                    if u == 1:
                        older_taps(2 * i + 1, 44 + 4 * i)
                    elif u == 2:
                        hidden(i)
                    elif u == 3:
                        hidden_low(i)
                add_up(2 * i + 2, 4)
                for u in range(UPR):
                    low(V + 3, u)
                    if u % 2 == 1:
                        add_down(V + 2, u // 2)

            with dve.Fori(0, BLOCKS - 1) as i:
                ff_block(i, False)
            ff_block(BLOCKS - 1, True)

        @block.gpsimd
        def _(pool):
            def prepare_fox(h):
                if h:
                    pool.wait_ge(scores, h)
                for i, (mat, r) in enumerate(((upper, 0), (upper, 1), (ones, 0))):
                    t = nc.gpsimd.tensor_scalar(prep[:, i * P:(i + 1) * P], mat,
                                                lf_keep[:, 8 * r + h:8 * r + h + 1], None, ALU.mult)
                t.then_inc(prep_ready, 1)

            def prepare_dil(h):
                pool.wait_ge(row_max, h)
                nc.gpsimd.tensor_copy(slope, smalls_sb[:, bass.ds(S_SLOPE + h - 8, 1)]).then_inc(slope_now, 1)
                pool.wait_ge(slope_now, h - 7)
                return nc.gpsimd.tensor_tensor(prep[:, :], neg_dist, slope.broadcast_to([P, 3 * P]), ALU.mult)

            def prepare(h):
                if h < 8:
                    prepare_fox(h)
                elif h < 12:
                    prepare_dil(h).then_inc(prep_ready, 1)

            def head_rms(nth):
                pool.wait_ge(ms_ready, nth + 1)
                nc.gpsimd.tensor_tensor(rs8, ms8, mhalf, ALU.pow).then_inc(rs_ready, 1)

            pool.wait_ge(smalls_in, 16)
            pool.wait_ge(ms_x, 1)
            nc.gpsimd.tensor_tensor(xrs, xms, mhalf[:, 0:2], ALU.pow).then_inc(rs_x, 1)
            head_rms(0)
            head_rms(1)
            pool.wait_ge(lf_ready, 1)
            pool.wait_ge(consts_in, 16)
            prepare(0)
            for g in range(1, GROUPS):
                h = 4 * (g - 1)
                prepare(h + 1)
                head_rms(2 * g)
                prepare(h + 2)
                prepare(h + 3)
                head_rms(2 * g + 1)
                prepare(h + 4)
            pool.wait_ge(qkt_ready, 16)
            pool.wait_ge(qkt_done, 16)
            pool.wait_ge(act_evac, 4)
            with pool.Fori(0, 4) as c:
                pool.wait_ge(o_ready, 12 + c)
                nc.gpsimd.tensor_copy(q_now, q_of(3)[:, bass.ds(c, 1), :])
                nc.gpsimd.tensor_copy(v_now, v_of(3)[:, :, bass.ds(c * P, P)])
                prepare_dil(12 + c).then_inc(prep_ready, 1)
            pool.wait_ge(ms_x, 2)
            nc.gpsimd.tensor_tensor(xrs, xms, mhalf[:, 0:2], ALU.pow).then_inc(rs_x, 1)


def _constants():
    c = np.zeros((P, C_N), np.float32)
    i, s = np.arange(P)[:, None], np.arange(P)[None, :]
    c[:, C_U:C_U + P] = i <= s
    c[:, C_M:C_M + P] = 1.0
    c[:, C_M + P:C_M + 2 * P] = i > s
    for n, d in enumerate((i - s, i - s + P, i - s)):
        at = slice(n * P, (n + 1) * P)
        n_patterns = ((d >= 0) & (d <= 128)) * 1 + ((d >= 0) & (d % 4 == 0)) * 1 + ((d >= 0) & (d % 16 == 0)) * 1
        c[:, C_MASK:C_MASK + 3 * P][:, at] = np.where(d >= 0, 0.0, NEG)
        c[:, C_ND:C_ND + 3 * P][:, at] = np.where(n_patterns > 0, -d, -1e34)
        c[:, C_CNT:C_CNT + 3 * P][:, at] = n_patterns
    return c


def kernel(x, g_attn, w_in, b_forget, g_q_fox, g_k_fox, g_q_dil, g_k_dil, w_br_fox, w_br_dil, w_out, g_ffn,
           w_up, w_conv, b_conv, w_down):
    import concourse.bacc as bacc
    from concourse.bass_utils import run_bass_kernel_spmd

    def tiles(v):
        return np.asarray(v).reshape(-1, P).T

    gq = [np.asarray(a)[0] for a in (g_q_fox, g_k_fox, g_q_dil, g_k_dil)]
    blocks = []
    for g in range(GROUPS):
        for m in range(2):
            blocks.append(gq[2 * (g // 2) + m][4 * (g % 2):4 * (g % 2) + 4].T)
    slopes = np.asarray(2.0 ** (-np.arange(1, 9)), np.float32)
    smalls = np.ascontiguousarray(np.concatenate(
        [np.eye(P, dtype=np.float32), tiles(np.asarray(g_attn)[0]), tiles(np.asarray(g_ffn)[0])] + blocks
        + [tiles(np.asarray(w_conv)[0, t]) for t in range(3)] + [tiles(np.asarray(b_conv)[0])]
        + [np.broadcast_to(np.asarray(b_forget)[0], (P, 8))] * 2
        + [np.broadcast_to(slopes, (P, 8)), np.full((P, 8), -0.5, np.float32)], axis=1))
    assert smalls.shape == (P, S_N)
    arrays = {"x": np.asarray(x), "smalls": smalls, "consts": _constants(), "w_in": np.asarray(w_in)[0],
              "w_fox": np.asarray(w_br_fox)[0], "w_dil": np.asarray(w_br_dil)[0], "w_out": np.asarray(w_out)[0],
              "w_up": np.asarray(w_up)[0], "w_down": np.asarray(w_down)[0]}
    nc = bacc.Bacc("TRN2", target_bir_lowering=False, num_devices=1)
    f32 = mybir.dt.float32
    aps = [nc.dram_tensor(n, a.shape, f32, kind="ExternalInput").ap() for n, a in arrays.items()]
    aps.append(nc.dram_tensor("out", (1, SEQ, DM), f32, kind="ExternalOutput").ap())
    decoder_layer(nc, *aps)
    r = run_bass_kernel_spmd(nc, [arrays], core_ids=[0])
    return r.results[0]["out"]
```

```python
import numpy as np
from contextlib import ExitStack

import concourse.bass as bass
from concourse import mybir

P = 128
SEQ = 256
RT = SEQ // P
DM = 2048
HD = 128
NHEADS = 16
D_FF = 5632
NB = 512
KU = 2
UNIT = KU * NB
UPR = 8
KT = DM // P
RAW_SLOTS = 4
EPS = 1e-6
NEG = -1e30
GROUPS = 4
X_SLOTS = (3, 5)
WARM_UP = 9
GATE0 = 12
BR0 = 20
OUT0 = 24
FF0 = 28
BLOCKS = D_FF // NB
CT = NB // P
V_PREV = FF0 + 1 + 3 * (BLOCKS - 2)
G_LAST, V_LAST, D_PREV, D_LAST = V_PREV + 1, V_PREV + 2, V_PREV + 3, V_PREV + 4
FA_COL = 3 * 1024
DIL_COL = FA_COL + 8
GATE_COL = DIL_COL + 3 * 1024

S_ID = 0
S_GATT = S_ID + P
S_GFFN = S_GATT + KT
S_GQK = S_GFFN + KT
S_MHALF = S_GQK + 32
S_SEL = S_MHALF + 8
S_WC = S_SEL + 8
S_BC = S_WC + 3 * 88
S_BF = S_BC + 88
S_SLOPE = S_BF + 8
S_N = S_SLOPE + 8
WF_PAD = P - 16
C_U = 0
C_M = C_U + P
C_MASK = C_M + 2 * P
C_ND = C_MASK + 3 * P
C_CNT = C_ND + 3 * P
C_N = C_CNT + 3 * P


def decoder_layer(nc, x, x_t, smalls, consts, w_in, w_fox, w_dil, w_out, w_up, w_down, out):
    f32 = mybir.dt.float32
    f32r = mybir.dt.float32r
    ALU = mybir.AluOpType
    ACT = mybir.ActivationFunctionType
    AX = mybir.AxisListType

    def rows_of(w):
        return w.rearrange("(k p) n -> p k n", p=P)

    x_rows = x.rearrange("b (r p) n -> p (b r) n", p=P)
    out_rows = out.rearrange("b (r p) n -> p (b r) n", p=P)
    w_in_v, w_fox_v, w_dil_v = rows_of(w_in), rows_of(w_fox), rows_of(w_dil)
    w_out_v, w_up_v, w_down_v = rows_of(w_out), rows_of(w_up), rows_of(w_down)

    ctx = ExitStack()
    with ctx:
        def sb(name, shape, dt=f32):
            return ctx.enter_context(nc.sbuf_tensor(name, shape, dt))

        def sem(name):
            return ctx.enter_context(nc.semaphore(name))

        raw = sb("raw", [P, RAW_SLOTS, UNIT])
        w_hi = sb("w_hi", [P, UPR, KU, NB], f32r)
        w_lo = sb("w_lo", [P, UPR, KU, NB], f32r)
        actA = sb("actA", [P, KT, 2 * SEQ], f32r)
        actB = sb("actB", [P, KT, 2 * SEQ], f32r)
        work = sb("work", [P, 8192])
        odd = sb("odd", [P, 3072])
        tmp = sb("tmp", [P, RT, NB])
        prob = sb("prob", [P, 3 * P])
        prob_t = sb("prob_t", [P, 3 * P])
        prep = sb("prep", [P, 3 * P])
        smalls_sb = sb("smalls_sb", [P, S_N])
        consts_sb = sb("consts_sb", [P, C_N])
        wf = sb("wf", [P, 16 * KT + WF_PAD], f32r)
        st = sb("st", [P, 96])
        acc = ctx.enter_context(nc.psum_tensor("acc", [P, 8, 512], f32))
        bank = [acc[:, i, :] for i in range(8)]

        ident = smalls_sb[:, S_ID:S_ID + P]
        upper = consts_sb[:, C_U:C_U + P]
        after = consts_sb[:, C_M:C_M + 2 * P]
        after_t = consts_sb[:, C_M + P:C_M + 2 * P]
        ones = consts_sb[:, C_M:C_M + P]
        mask = consts_sb[:, C_MASK:C_MASK + 3 * P]
        neg_dist = consts_sb[:, C_ND:C_ND + 3 * P]
        count = consts_sb[:, C_CNT:C_CNT + 3 * P]
        mhalf = smalls_sb[:, S_MHALF:S_MHALF + 8]

        xr = work[:, 4096:8192].rearrange("p (r n) -> p r n", r=RT)
        xt = work[:, 0:4096].rearrange("p (k s) -> p k s", k=KT)
        ga = work[:, 0:4096].rearrange("p (r n) -> p r n", r=RT)
        gb = work[:, 4096:8192].rearrange("p (r n) -> p r n", r=RT)
        wf_raw = odd[:, 0:128].rearrange("p (k n) -> p k n", k=KT)
        wf_k = wf[:, 0:16 * KT].rearrange("p (k c n) -> p k c n", k=KT, c=2)
        forget = odd[:, 128:128 + 3 * 16].rearrange("p (a n) -> p a n", a=3)
        fa_t = odd[0:16, 256:768]
        heads = (work, odd)

        def q_of(g):
            return heads[g % 2][:, 0:1024].rearrange("p (j s) -> p j s", j=4)

        def k_of(g):
            return heads[g % 2][:, 1024:2048].rearrange("p (j s) -> p j s", j=4)

        def v_of(g):
            return heads[g % 2][:, 2048:3072].rearrange("p (r n) -> p r n", r=RT)

        upad = work[:, 0:4 * 258].rearrange("p (j s) -> p j s", j=CT)
        conv = work[:, 1032:2056].rearrange("p (j s) -> p j s", j=CT)
        silu = work[:, 2056:3080].rearrange("p (j s) -> p j s", j=CT)
        q_now = tmp[:, 0, 0:SEQ]
        v_now = tmp[:, 0, SEQ:2 * SEQ].rearrange("p (r n) -> p r n", r=RT)
        tmp_j = tmp[:, :, :].rearrange("p r (a s) -> p (r a) s", a=2)
        rstd_row = odd[:, 0:SEQ]
        diag = odd[:, 256:512]
        square = odd[:, 512:1536].rearrange("p (r n) -> p r n", r=RT)

        ss8, ms8, rs8, rs8x = st[:, 0:8], st[:, 8:16], st[:, 16:24], st[:, 72:80]
        xrs8 = st[:, 80:88]
        xrs2 = st[:, 88:90]
        mx, nmx, den, rden = st[:, 24:26], st[:, 26:28], st[:, 28:30], st[:, 30:32]
        xss, xms, xrs = st[:, 32:34], st[:, 34:36], st[:, 36:38]
        ssp = st[:, 40:48]
        fz, fb, fn = (forget[:, i, :] for i in range(3))
        slope = st[:, 64:65]
        lf_keep = st[:, 48:64]

        x_in = [sem(f"x_in{r}") for r in range(RT)]
        xt_in = [sem(f"xt_in{u}") for u in range(UPR)]
        smalls_in, consts_in, wf_in, x_again, out_done = (
            sem("smalls_in"), sem("consts_in"), sem("wf_in"), sem("x_again"), sem("out_done"))
        first_tile, gains_in, tile_high, tile_split, warm_data = (
            sem("first_tile"), sem("gains_in"), sem("tile_high"), sem("tile_split"), sem("warm_data"))
        w_loaded = [sem(f"w_loaded{s}") for s in range(RAW_SLOTS)]
        hi_done, lo_done, used = sem("hi_done"), sem("lo_done"), sem("unit_used")
        sums_x, ms_x, rs_x, rs_x8 = sem("sums_x"), sem("ms_x"), sem("rs_x"), sem("rs_x8")
        h_hi, h_lo, ident_in, pad_done, rs_scaled = (
            sem("h_hi"), sem("h_lo"), sem("ident_in"), sem("pad_done"), sem("rs_scaled"))
        sq_ready, ms_ready, rs_ready, qn_done = sem("sq_ready"), sem("ms_ready"), sem("rs_ready"), sem("qn_done")
        qkt_ready, qkt_done, act_evac = sem("qkt_ready"), sem("qkt_done"), sem("act_evac")
        wf_split, fa_ready, fa_out, fa_rows, fa_arg, fa_exp, fa_ln, lf_ready = (
            sem("wf_split"), sem("fa_ready"), sem("fa_out"), sem("fa_rows"), sem("fa_arg"), sem("fa_exp"), sem("fa_ln"),
            sem("lf_ready"))
        prep_ready, scores, maxed, exped, normed = (
            sem("prep_ready"), sem("scores"), sem("maxed"), sem("exped"), sem("normed"))
        pt_ready, pt_copied, o_ready, o_hi, o_lo = (
            sem("pt_ready"), sem("pt_copied"), sem("o_ready"), sem("o_hi"), sem("o_lo"))
        fox_merged, merged, mt_ready, mt_hi, mt_lo = (
            sem("fox_merged"), sem("merged"), sem("mt_ready"), sem("mt_hi"), sem("mt_lo"))
        x2_done, x2_sq, x2t_ready, x2t_hi, x2t_lo = (
            sem("x2_done"), sem("x2_sq"), sem("x2t_ready"), sem("x2t_hi"), sem("x2t_lo"))
        diag_ready, bc_ready, bc_done = sem("diag_ready"), sem("bc_ready"), sem("bc_done")
        low_copied, up_added, u_ready, tap2, conv_done, silu_done = (
            sem("low_copied"), sem("up_added"), sem("u_ready"), sem("tap2"), sem("conv_done"), sem("silu_done"))
        a_ready, a_hi, a_lo, d_added = sem("a_ready"), sem("a_hi"), sem("a_lo"), sem("d_added")
        row_max, den_ready, rden_ready, dil_merged, tap1, ss_ready, fa_sum, fa_neg = (
            sem("row_max"), sem("den_ready"), sem("rden_ready"), sem("dil_merged"), sem("tap1"),
            sem("ss_ready"), sem("fa_sum"), sem("fa_neg"))
        biased, slope_now, warm, row0_done = sem("biased"), sem("slope_now"), sem("warm"), sem("row0_done")
        block = ctx.enter_context(nc.Block())

        def turn_slot(g):
            return 3 if g < 3 else 4

        def turned_at(g):
            q_slots = (12, 14) if g else (14, 15)
            return {q_slots[0]: (0, 0), q_slots[1]: (0, 1), 20: (1, 0), 22: (1, 1)}

        @block.sync
        def _(sp):
            def load(R, u, src):
                n = UPR * R + u
                if not (isinstance(R, int) and n < RAW_SLOTS):
                    if isinstance(R, int) and n == RAW_SLOTS:
                        sp.wait_ge(tile_split, KU)
                    else:
                        sp.wait_ge(lo_done, n - RAW_SLOTS)
                s = u % RAW_SLOTS
                sp.dma_start(raw[:, s, :].rearrange("p (k n) -> p k n", k=KU), src).then_inc(w_loaded[s], 16)

            def round_of(R, w, col):
                for u in range(UPR):
                    load(R, u, w[:, KU * u:KU * u + KU, bass.ds(col, NB)])

            def down_round(R, blk):
                for u in range(UPR):
                    load(R, u, w_down_v[:, bass.ds(CT * blk + KU * (u % 2), KU), (u // 2) * NB:(u // 2 + 1) * NB])

            for u in range(UPR):
                k = slice(KU * u, KU * u + KU)
                if u == 0:
                    sp.dma_start(raw[:, 0, 0:NB], w_in_v[:, 0, 0:NB]).then_inc(first_tile, 16)
                    sp.dma_start(xt[:, k, :], x_t[:, k, :]).then_inc(xt_in[0], 16)
                    sp.dma_start(raw[:, 0, NB:2 * NB], w_in_v[:, 1, 0:NB]).then_inc(w_loaded[0], 16)
                else:
                    sp.dma_start(xt[:, k, :], x_t[:, k, :]).then_inc(xt_in[u], 16)
                    load(0, u, w_in_v[:, k, 0:NB])
            sp.dma_start(xr[:, 0, :], x_rows[:, 0, :]).then_inc(x_in[0], 16)
            for u in range(UPR):
                load(1, u, w_in_v[:, KU * u:KU * u + KU, 1024:1024 + NB])
                if u == 1:
                    sp.dma_start(xr[:, 1, :], x_rows[:, 1, :]).then_inc(x_in[1], 16)
            sp.dma_start(smalls_sb[:, S_WC:S_N], smalls[:, S_WC:S_N]).then_inc(smalls_in, 16)
            for g in range(GROUPS):
                base = (0 if g < 2 else DIL_COL) + (g % 2) * NB
                for m in range(3):
                    if 3 * g + m > 1:
                        round_of(3 * g + m, w_in_v, base + 1024 * m)
            with sp.Fori(0, 4) as c:
                round_of(GATE0 + 2 * c, w_in_v, GATE_COL + NB * c)
                round_of(GATE0 + 1 + 2 * c, w_in_v, GATE_COL + DM + NB * c)
            with sp.Fori(0, 4) as c:
                for u in range(UPR):
                    w = w_fox_v if u < 4 else w_dil_v
                    load(BR0 + c, u, w[:, KU * (u % 4):KU * (u % 4) + KU, bass.ds(NB * c, NB)])
            with sp.Fori(0, 4) as c:
                round_of(OUT0 + c, w_out_v, NB * c)
            round_of(FF0, w_up_v, 0)
            with sp.Fori(0, BLOCKS - 2) as i:
                round_of(FF0 + 1 + 3 * i, w_up_v, D_FF + NB * i)
                round_of(FF0 + 2 + 3 * i, w_up_v, NB + NB * i)
                down_round(FF0 + 3 + 3 * i, i)
            last = BLOCKS - 1
            round_of(V_PREV, w_up_v, D_FF + NB * (last - 1))
            round_of(G_LAST, w_up_v, NB * last)
            round_of(V_LAST, w_up_v, D_FF + NB * last)
            down_round(D_PREV, last - 1)
            down_round(D_LAST, last)
            for c in range(4):
                for r in range(RT):
                    sp.wait_ge(d_added, 1 + 8 * last + 2 * c + r + 1)
                    sp.dma_start(out_rows[:, r, c * NB:(c + 1) * NB], xr[:, r, c * NB:(c + 1) * NB])\
                        .then_inc(out_done, 16)
            sp.wait_ge(out_done, 16 * 4 * RT)

        @block.tensor
        def _(pe):
            def rows_unit(R, u, act, kts, banks, first, last, row0=None):
                pe.wait_ge(lo_done, UPR * R + u)
                for r in range(RT):
                    for k, kt in enumerate(kts):
                        a_h = act[:, kt, r * P:(r + 1) * P]
                        a_l = act[:, kt, SEQ + r * P:SEQ + (r + 1) * P]
                        o = banks[r][:, :]
                        nc.tensor.matmul(o, lhsT=a_h, rhs=w_hi[:, u, k, :], start=first and k == 0, stop=False)
                        nc.tensor.matmul(o, lhsT=a_h, rhs=w_lo[:, u, k, :], start=False, stop=False)
                        mm = nc.tensor.matmul(o, lhsT=a_l, rhs=w_hi[:, u, k, :], start=False,
                                              stop=last and k == KU - 1)
                    if row0 is not None and r == 0:
                        mm.then_inc(row0, 1)
                mm.then_inc(used, 1)

            def cols_unit(R, u, banks):
                pe.wait_ge(lo_done, UPR * R + u)
                for k in range(KU):
                    kt = KU * u + k
                    for j in range(CT):
                        hi_w, lo_w = w_hi[:, u, k, j * P:(j + 1) * P], w_lo[:, u, k, j * P:(j + 1) * P]
                        if kt == 0:
                            nc.tensor.matmul(banks[j][:, :], lhsT=hi_w, rhs=actB[:, kt, :], start=True, stop=False)
                        mm = nc.tensor.matmul(banks[j][:, SEQ:], lhsT=lo_w, rhs=actB[:, kt, 0:SEQ],
                                              start=False, stop=False)
                        if kt > 0:
                            mm = nc.tensor.matmul(banks[j][:, :], lhsT=hi_w, rhs=actB[:, kt, :], start=False,
                                                  stop=kt == KT - 1)
                mm.then_inc(used, 1)

            def transpose_block(src, banks, ready):
                for b in range(2):
                    for j in range(2):
                        for r in range(RT):
                            t = nc.tensor.transpose(banks[b][:, j * SEQ + r * P:j * SEQ + (r + 1) * P],
                                                    src(r, (2 * b + j) * P), ident)
                    t.then_inc(ready, 1)

            def transpose_heads(nth, half):
                pe.wait_ge(qn_done, nth + 1)
                if nth or half:
                    pe.wait_ge(qkt_done, 2 * nth + half)
                for j in range(2):
                    for r in range(RT):
                        col = (2 * half + j) * P
                        t = nc.tensor.transpose(bank[7][:, j * SEQ + r * P:j * SEQ + (r + 1) * P],
                                                tmp[:, r, col:col + P], ident)
                t.then_inc(qkt_ready, 1)

            def attend_scores(h, q, k, fox):
                s = bank[4]
                pe.wait_ge(prep_ready, h + 1)
                nc.tensor.matmul(s[:, 0:P], lhsT=q[:, 0:P], rhs=k(0, P), start=True, stop=not fox)
                if fox:
                    nc.tensor.matmul(s[:, 0:P], lhsT=prep[:, 0:P], rhs=after_t, start=False, stop=True)
                mm = nc.tensor.matmul(s[:, P:3 * P], lhsT=q[:, P:2 * P], rhs=k(0, SEQ), start=True, stop=not fox)
                if fox:
                    nc.tensor.matmul(s[:, P:2 * P], lhsT=prep[:, 2 * P:3 * P], rhs=after_t, start=False, stop=False)
                    mm = nc.tensor.matmul(s[:, P:3 * P], lhsT=prep[:, P:2 * P], rhs=after, start=False, stop=True)
                mm.then_inc(scores, 1)

            def attend_transpose(h):
                pe.wait_ge(normed, h + 1)
                for i in range(3):
                    t = nc.tensor.transpose(bank[5][:, i * P:(i + 1) * P], prob[:, i * P:(i + 1) * P], ident)
                t.then_inc(pt_ready, 1)

            def attend_values(h, v0, v1):
                pe.wait_ge(pt_copied, h + 1)
                if not (isinstance(h, int) and h == 0):
                    pe.wait_ge(o_lo, h)
                nc.tensor.matmul(bank[6][:, 0:SEQ], lhsT=v0, rhs=prob_t[:, 0:2 * P], start=True, stop=False)
                nc.tensor.matmul(bank[6][:, P:SEQ], lhsT=v1, rhs=prob_t[:, 2 * P:3 * P],
                                 start=False, stop=True).then_inc(o_ready, 1)

            def first_unit(banks):
                for kt in range(KU):
                    pe.wait_ge(tile_split, kt + 1)
                    pe.wait_ge(h_lo, kt + 1)
                    for r in range(RT):
                        a_h = actA[:, kt, r * P:(r + 1) * P]
                        a_l = actA[:, kt, SEQ + r * P:SEQ + (r + 1) * P]
                        nc.tensor.matmul(banks[r][:, :], lhsT=a_h, rhs=w_hi[:, 0, kt, :], start=kt == 0, stop=False)
                        nc.tensor.matmul(banks[r][:, :], lhsT=a_h, rhs=w_lo[:, 0, kt, :], start=False, stop=False)
                        mm = nc.tensor.matmul(banks[r][:, :], lhsT=a_l, rhs=w_hi[:, 0, kt, :], start=False, stop=False)
                mm.then_inc(used, 1)

            pe.wait_ge(warm_data, 1)
            for _ in range(WARM_UP):
                nc.tensor.matmul(bank[7][:, :], lhsT=actB[:, KT - 1, 0:P], rhs=actB[:, KT - 1, :], start=True, stop=True)

            for g in range(GROUPS):
                turned = turned_at(g)
                for m in range(3):
                    R = 3 * g + m
                    banks = bank[2 * (R % 2):2 * (R % 2) + 2]
                    if R >= 2:
                        before = R - 2
                        if before % 3 == 2:
                            pe.wait_ge(act_evac, before // 3 + 1)
                        else:
                            pe.wait_ge(qn_done, 2 * (before // 3) + before % 3 + 1)
                    for u in range(UPR):
                        if R == 0 and u == 0:
                            first_unit(banks)
                        else:
                            if R == 0:
                                pe.wait_ge(h_lo, KU * u + 2)
                            rows_unit(R, u, actA, (KU * u, KU * u + 1), banks, u == 0, u == UPR - 1)
                        slot = UPR * m + u
                        j, at = slot // 6, slot % 6
                        h = 4 * (g - 1) + j
                        if g > 0 and at == 1:
                            if j == 0:
                                pe.wait_ge(qkt_done, 4 * g)
                                pe.wait_ge(act_evac, g)
                                pe.wait_ge(consts_in, 16)
                            attend_scores(h, q_of(g - 1)[:, j, :], lambda a, b: k_of(g - 1)[:, j, a:b], g <= 2)
                        elif g > 0 and at == turn_slot(g):
                            attend_transpose(h)
                        elif g > 0 and at == 5:
                            v = v_of(g - 1)
                            attend_values(h, v[:, 0, j * P:(j + 1) * P], v[:, 1, j * P:(j + 1) * P])
                        if slot in turned:
                            transpose_heads(2 * g + turned[slot][0], turned[slot][1])
                        if g == 0 and slot == 18:
                            pe.wait_ge(wf_split, 2)
                            pe.wait_ge(pad_done, 1)
                            for kt in range(KT):
                                mm = nc.tensor.matmul(bank[6][:, :], lhsT=wf[:, 16 * kt:16 * kt + P],
                                                      rhs=actA[:, kt, :], start=kt == 0, stop=kt == KT - 1)
                            mm.then_inc(fa_ready, 1)
                        if g == 0 and slot == 20:
                            pe.wait_ge(fa_out, 1)
                            for r in range(RT):
                                for n in range(2):
                                    col = SEQ * n + r * P
                                    mm = nc.tensor.matmul(bank[5][:, 8 * r:8 * r + 8], lhsT=fa_t[:, col:col + P],
                                                          rhs=smalls_sb[0:16, S_SEL:S_SEL + 8],
                                                          start=n == 0, stop=n == 1)
                            mm.then_inc(fa_rows, 1)

            pe.wait_ge(qn_done, 2 * GROUPS)
            with pe.Fori(0, 4) as c:
                for m in range(2):
                    R = GATE0 + m + 2 * c
                    pe.wait_ge(act_evac, 3 + m + 2 * c)
                    for u in range(UPR):
                        rows_unit(R, u, actA, (KU * u, KU * u + 1), bank[2 * m:2 * m + 2], u == 0, u == UPR - 1)
                        if m == 0 and u == 1:
                            attend_scores(12 + c, q_now, lambda a, b: odd[:, bass.ds(1024 + SEQ * c + a, b - a)], False)
                        elif m == 0 and u == 4:
                            attend_transpose(12 + c)
                        elif m == 0 and u == 7:
                            attend_values(12 + c, v_now[:, 0, :], v_now[:, 1, :])

            def branch_round(c):
                pe.wait_ge(act_evac, 4 + 7)
                for u in range(UPR):
                    pair = bank[0:2] if u < 4 else bank[2:4]
                    rows_unit(BR0 + c, u, actB, (KU * u, KU * u + 1), pair, u % 4 == 0, u % 4 == 3)
                    yield u

            pe.wait_ge(o_lo, NHEADS)
            for u in branch_round(0):
                if u == 3:
                    pe.wait_ge(act_evac, 4 + 8)
            with pe.Fori(1, 4) as c:
                pe.wait_ge(fox_merged, c)
                for u in branch_round(c):
                    if u == 2:
                        pe.wait_ge(merged, c)
                        transpose_block(lambda r, col: tmp[:, r, col:col + P], bank[4:6], mt_ready)

            for c in range(4):
                R, banks = OUT0 + c, bank[2 * (c % 2):2 * (c % 2) + 2]
                if c == 0:
                    pe.wait_ge(fox_merged, 4)
                    pe.wait_ge(mt_lo, 6)
                elif c == 1:
                    pe.wait_ge(merged, 4)
                else:
                    pe.wait_ge(x2_done, c - 1)
                for u in range(UPR):
                    if c == 0 and u == 6:
                        pe.wait_ge(mt_lo, 8)
                    rows_unit(R, u, actA, (KU * u, KU * u + 1), banks, u == 0, u == UPR - 1)
                    if u == 2 and c == 0:
                        pe.wait_ge(merged, 4)
                        transpose_block(lambda r, col: tmp[:, r, col:col + P], bank[4:6], mt_ready)
                    elif u == 2:
                        pe.wait_ge(x2_done, c)
                        if c > 1:
                            pe.wait_ge(x2t_lo, 4 * (c - 1))
                        transpose_block(lambda r, col: xr[:, r, (c - 1) * NB + col:(c - 1) * NB + col + P],
                                        bank[4:6], x2t_ready)

            pe.wait_ge(x2t_lo, 12)
            for u in range(UPR):
                if u == 6:
                    pe.wait_ge(x2t_lo, 16)
                cols_unit(FF0, u, bank[4:8])
                if u == 2:
                    pe.wait_ge(x2_done, 4)
                    transpose_block(lambda r, col: xr[:, r, 3 * NB + col:3 * NB + col + P], bank[0:2], x2t_ready)
                if u == 5:
                    pe.wait_ge(diag_ready, 1)
                    nc.tensor.matmul(bank[2][:, 0:SEQ], lhsT=ones, rhs=diag, start=True, stop=True)\
                        .then_inc(bc_ready, 1)
            pe.wait_ge(bc_done, 1)

            def up_round(R, banks):
                for u in range(UPR):
                    cols_unit(R, u, banks)

            def down_unit(R, u, first_kt, first_bank, row0=None):
                c, k = u // 2, first_kt + KU * (u % 2)
                pair = (first_bank + 2 * c) % 8
                rows_unit(R, u, actA, (k, k + 1), bank[pair:pair + 2], u % 2 == 0, u % 2 == 1, row0)

            with pe.Fori(0, BLOCKS - 2) as i:
                up_round(FF0 + 1 + 3 * i, bank[0:4])
                pe.wait_ge(d_added, 1 + 8 * i)
                up_round(FF0 + 2 + 3 * i, bank[4:8])
                pe.wait_ge(a_lo, i + 1)
                pe.wait_ge(up_added, 2 * i + 2)
                for u in range(UPR):
                    if u == 4:
                        pe.wait_ge(up_added, 2 * i + 3)
                    if u == 6:
                        pe.wait_ge(d_added, 1 + 8 * i + 4)
                    down_unit(FF0 + 3 + 3 * i, u, 0, 0)
            up_round(V_PREV, bank[0:4])
            pe.wait_ge(d_added, 1 + 8 * (BLOCKS - 2))
            up_round(G_LAST, bank[4:8])
            pe.wait_ge(up_added, 2 * BLOCKS - 2)
            up_round(V_LAST, bank[0:4])
            pe.wait_ge(a_lo, BLOCKS - 1)
            pe.wait_ge(up_added, 2 * BLOCKS - 1)
            for u in range(UPR):
                if u == 4:
                    pe.wait_ge(up_added, 2 * BLOCKS)
                down_unit(D_PREV, u, 0, 4)
            pe.wait_ge(a_lo, BLOCKS)
            for u in range(UPR):
                if u % 2 == 0:
                    pe.wait_ge(d_added, 1 + 8 * (BLOCKS - 2) + u + 2)
                down_unit(D_LAST, u, CT, 4, row0_done if u == UPR - 1 else None)

        @block.scalar
        def _(act):
            def high(R, u):
                act.wait_ge(w_loaded[u % RAW_SLOTS], 16 * (2 * R + u // RAW_SLOTS + 1))
                if not (isinstance(R, int) and R == 0):
                    act.wait_ge(used, UPR * (R - 1) + u + 1)
                nc.scalar.activation(w_hi[:, u, :, :], raw[:, u % RAW_SLOTS, :].rearrange("p (k n) -> p k n", k=KU),
                                     ACT.Copy).then_inc(hi_done, 1)

            def exps(h):
                act.wait_ge(maxed, h + 1)
                nc.scalar.activation(prob[:, 0:P], prob[:, 0:P], ACT.Exp, bias=nmx[:, 0:1],
                                     accum_out=den[:, 0:1])
                nc.scalar.activation(prob[:, P:3 * P], prob[:, P:3 * P], ACT.Exp, bias=nmx[:, 1:2],
                                     accum_out=den[:, 1:2]).then_inc(exped, 1)

            def copy_pt(h):
                act.wait_ge(pt_ready, h + 1)
                nc.scalar.activation(prob_t[:, :], bank[5][:, 0:3 * P], ACT.Copy).then_inc(pt_copied, 1)

            def out_high(h):
                act.wait_ge(o_ready, h + 1)
                dst = actB[:, h, 0:SEQ] if isinstance(h, int) else actB[:, bass.ds(h, 1), 0:SEQ]
                nc.scalar.activation(dst, bank[6][:, 0:SEQ], ACT.Copy).then_inc(o_hi, 1)

            def merged_high(c):
                for b in range(2):
                    act.wait_ge(mt_ready, 2 * c + b + 1)
                    kt = 4 * c + 2 * b
                    nc.scalar.activation(actA[:, bass.ds(kt, 2), 0:SEQ],
                                         bank[4 + b][:, :].rearrange("p (j s) -> p j s", j=2),
                                         ACT.Copy).then_inc(mt_hi, 1)

            def x2_squares(c):
                act.wait_ge(x2_done, c + 1)
                if c:
                    act.wait_ge(x2_sq, RT * c)
                for r in range(RT):
                    nc.scalar.activation(square[:, r, :], xr[:, r, c * NB:(c + 1) * NB], ACT.Square,
                                         accum_out=ssp[:, 4 * r + c:4 * r + c + 1]).then_inc(x2_sq, 1)

            def x2t_high(c, banks):
                for b in range(2):
                    act.wait_ge(x2t_ready, 2 * c + b + 1)
                    for j in range(2):
                        kt = 4 * c + 2 * b + j
                        nc.scalar.activation(actB[:, kt, 0:SEQ], banks[b][:, j * SEQ:(j + 1) * SEQ], ACT.Copy,
                                             scale=smalls_sb[:, S_GFFN + kt:S_GFFN + kt + 1]).then_inc(x2t_hi, 1)

            act.dma_start(smalls_sb[:, S_GATT:S_GFFN], smalls[:, S_GATT:S_GFFN]).then_inc(gains_in, 16)
            act.wait_ge(warm, 1)
            nc.scalar.activation(st[:, 90:91], st[:, 91:92], ACT.Square).then_inc(warm, 1)
            for u in range(UPR):
                if u > 0:
                    act.wait_ge(xt_in[u], 16)
                for kt in (KU * u, KU * u + 1):
                    if u == 0:
                        act.wait_ge((first_tile, w_loaded[0])[kt], 16)
                        nc.scalar.activation(w_hi[:, 0, kt, :], raw[:, 0, kt * NB:(kt + 1) * NB], ACT.Copy)\
                            .then_inc(tile_high, 1)
                        if kt == 0:
                            act.wait_ge(gains_in, 16)
                            act.wait_ge(xt_in[0], 16)
                    nc.scalar.activation(actA[:, kt, 0:SEQ], xt[:, kt, :], ACT.Copy,
                                         scale=smalls_sb[:, S_GATT + kt:S_GATT + kt + 1]).then_inc(h_hi, 1)
                if u > 0:
                    high(0, u)
                if u == 3:
                    act.dma_start(smalls_sb[:, 0:S_GATT], smalls[:, 0:S_GATT]).then_inc(ident_in, 16)
                    act.dma_start(smalls_sb[:, S_GFFN:S_WC], smalls[:, S_GFFN:S_WC]).then_inc(ident_in, 16)

            act.wait_ge(ident_in, 32)
            for g in range(GROUPS):
                turned = turned_at(g) if g else {11: (0, 0), 12: (0, 1), 20: (1, 0), 22: (1, 1)}
                for m in range(3):
                    R = 3 * g + m
                    pair = 2 * (R % 2)
                    for u in range(UPR):
                        high(R + 1, u)
                        slot = UPR * m + u
                        j, at = slot // 6, slot % 6
                        h = 4 * (g - 1) + j
                        if g > 0 and at == 1:
                            exps(h)
                        elif g > 0 and at == turn_slot(g):
                            copy_pt(h)
                        elif g > 0 and at == 5:
                            out_high(h)
                        if slot in turned:
                            nth = 2 * g + turned[slot][0]
                            act.wait_ge(qkt_ready, 2 * nth + turned[slot][1] + 1)
                            dst = (q_of(g), k_of(g))[turned[slot][0]]
                            for jj in range(2):
                                head = 2 * turned[slot][1] + jj
                                col = S_GQK + 4 * nth + head
                                t = nc.scalar.activation(dst[:, head, :], bank[7][:, jj * SEQ:(jj + 1) * SEQ],
                                                         ACT.Copy, scale=smalls_sb[:, col:col + 1])
                            t.then_inc(qkt_done, 1)
                        if u == (UPR - 1 if R else UPR - 2):
                            act.wait_ge(used, UPR * R + UPR)
                            if m < 2:
                                if R:
                                    act.wait_ge(qkt_ready, 2 * (2 * g + m))
                                if R == 0:
                                    act.wait_ge(rs_x, 1)
                                for r in range(RT):
                                    t = nc.scalar.activation(tmp[:, r, :], bank[pair + r][:, :], ACT.Square,
                                                             scale=xrs[:, r:r + 1])
                                t.then_inc(sq_ready, 1)
                            else:
                                for r in range(RT):
                                    t = nc.scalar.activation(v_of(g)[:, r, :], bank[pair + r][:, :], ACT.Copy,
                                                             scale=xrs[:, r:r + 1])
                                t.then_inc(act_evac, 1)
                        if g == 0 and slot in X_SLOTS:
                            r = X_SLOTS.index(slot)
                            act.wait_ge(x_in[r], 16)
                            nc.scalar.activation(xr[:, r, :], xr[:, r, :], ACT.Square, accum_out=xss[:, r:r + 1])\
                                .then_inc(sums_x, 1)
                        if g == 0 and slot == 8:
                            act.dma_start(wf_raw, w_in_v[:, :, FA_COL:FA_COL + 8]).then_inc(wf_in, 16)
                        if g == 0 and slot == 10:
                            act.wait_ge(wf_in, 16)
                            nc.scalar.activation(wf_k[:, :, 0, :], wf_raw, ACT.Copy).then_inc(wf_split, 1)
                        if g == 0 and slot == 15:
                            act.dma_start(consts_sb[:, :], consts).then_inc(consts_in, 16)
                        if g == 0 and slot == 19:
                            act.wait_ge(fa_ready, 1)
                            nc.scalar.activation(fa_t, bank[6][0:16, :], ACT.Copy).then_inc(fa_out, 1)
                        if g == 0 and slot == 21:
                            act.wait_ge(fa_arg, 1)
                            nc.scalar.activation(fn, fn, ACT.Exp).then_inc(fa_exp, 1)
                            act.wait_ge(fa_exp, 1)
                            nc.scalar.activation(fn, fn, ACT.Ln, bias=1.0).then_inc(fa_ln, 1)

            with act.Fori(0, 4) as c:
                for m in range(2):
                    R = GATE0 + m + 2 * c
                    for u in range(UPR):
                        high(R + 1, u)
                        if m == 0 and u == 1:
                            exps(12 + c)
                        elif m == 0 and u == 4:
                            copy_pt(12 + c)
                        elif m == 0 and u == 7:
                            out_high(12 + c)
                        if u == UPR - 1:
                            act.wait_ge(used, UPR * R + UPR)
                            for r in range(RT):
                                t = nc.scalar.activation((ga, gb)[m][:, r, bass.ds(c * NB, NB)],
                                                         bank[2 * m + r][:, :], ACT.Sigmoid,
                                                         scale=xrs[:, r:r + 1])
                            t.then_inc(act_evac, 1)

            for u in range(UPR):
                high(BR0 + 1, u)
            with act.Fori(1, 4) as c:
                for u in range(UPR):
                    high(BR0 + 1 + c, u)
                    if u == 2:
                        merged_high(c - 1)

            for c in range(4):
                R = OUT0 + c
                for u in range(UPR):
                    high(R + 1, u)
                    if u == 1 and c == 0:
                        act.wait_ge(merged, 4)
                        act.dma_start(xr[:, :, :], x_rows).then_inc(x_again, 16)
                    if u == 2 and c == 0:
                        merged_high(3)
                    elif u == 2:
                        x2t_high(c - 1, bank[4:6])
                x2_squares(c)

            def low_copy(R, q, b0):
                act.wait_ge(used, UPR * R + UPR)
                nc.scalar.activation(tmp_j, acc[:, b0:b0 + CT, SEQ:2 * SEQ], ACT.Copy).then_inc(low_copied, 1)

            def newest_tap(q, ct):
                act.wait_ge(u_ready, q + 1)
                for j in range(CT):
                    t = nc.scalar.activation(conv[:, j, :], upad[:, j, 2:2 + SEQ], ACT.Identity,
                                             scale=smalls_sb[:, bass.ds(S_WC + 2 * 88 + ct + j, 1)],
                                             bias=smalls_sb[:, bass.ds(S_BC + ct + j, 1)])
                t.then_inc(tap2, 1)

            def gate_silu(q):
                act.wait_ge(conv_done, q + 1)
                nc.scalar.activation(silu, conv, ACT.Silu).then_inc(silu_done, 1)

            def hidden_high(i, first_kt=0):
                act.wait_ge(a_ready, i + 1)
                nc.scalar.activation(actA[:, first_kt:first_kt + CT, 0:SEQ], tmp_j, ACT.Copy).then_inc(a_hi, 1)

            for u in range(UPR):
                high(FF0 + 1, u)
                if u == 2:
                    x2t_high(3, bank[0:2])
                if u == 5:
                    act.wait_ge(bc_ready, 1)
                    nc.scalar.activation(rstd_row, bank[2][:, 0:SEQ], ACT.Copy).then_inc(bc_done, 1)
            low_copy(FF0, 0, 4)

            def value_round(V, i):
                for u in range(UPR):
                    high(V + 1, u)
                    if u == 0:
                        newest_tap(2 * i, 4 * i)
                    elif u == 2:
                        gate_silu(2 * i)
                act.wait_ge(u_ready, 2 * i + 1)
                low_copy(V, 2 * i + 1, 0)

            def gate_round(G, i):
                for u in range(UPR):
                    high(G + 1, u)
                    if u == 0:
                        newest_tap(2 * i + 1, 44 + 4 * i)
                    elif u == 3:
                        hidden_high(i)
                act.wait_ge(a_lo, i + 1)
                low_copy(G, 2 * i + 2, 4)

            with act.Fori(0, BLOCKS - 2) as i:
                value_round(FF0 + 1 + 3 * i, i)
                gate_round(FF0 + 2 + 3 * i, i)
                for u in range(UPR):
                    high(FF0 + 4 + 3 * i, u)
            value_round(V_PREV, BLOCKS - 2)
            gate_round(G_LAST, BLOCKS - 2)
            value_round(V_LAST, BLOCKS - 1)
            for u in range(UPR):
                high(D_LAST, u)
                if u == 0:
                    newest_tap(2 * BLOCKS - 1, 44 + 4 * (BLOCKS - 1))
                elif u == 3:
                    hidden_high(BLOCKS - 1, CT)

        @block.vector
        def _(dve):
            def low(R, u):
                dve.wait_ge(hi_done, UPR * R + u)
                nc.vector.tensor_tensor(w_lo[:, u, :, :],
                                        raw[:, u % RAW_SLOTS, :].rearrange("p (k n) -> p k n", k=KU),
                                        w_hi[:, u, :, :].bitcast(f32), ALU.subtract).then_inc(lo_done, 1)

            def softmax_head(h, bias, dil):
                dve.wait_ge(scores, h + 1)
                parts = ((0, P), (P, 3 * P))
                if dil:
                    nc.vector.tensor_tensor(prob[:, :], bank[4][:, 0:3 * P], bias[:, :], ALU.add).then_inc(biased, 1)
                    dve.wait_ge(biased, h - 7)
                for i, (a, b) in enumerate(parts):
                    if dil:
                        t = nc.vector.reduce_max(mx[:, i:i + 1], prob[:, a:b], AX.X)
                    else:
                        t = nc.vector.tensor_tensor_reduce(out=prob[:, a:b], in0=bank[4][:, a:b], in1=bias[:, a:b],
                                                           scale=1.0, scalar=-3.0e38, op0=ALU.add, op1=ALU.max,
                                                           accum_out=mx[:, i:i + 1])
                t.then_inc(row_max, 1)
                dve.wait_ge(row_max, h + 1)
                nc.vector.tensor_scalar(nmx, mx, -1.0, None, ALU.mult).then_inc(maxed, 1)
                dve.wait_ge(exped, h + 1)
                if dil:
                    for i, (a, b) in enumerate(parts):
                        t = nc.vector.tensor_tensor_reduce(out=prob[:, a:b], in0=prob[:, a:b], in1=count[:, a:b],
                                                           scale=1.0, scalar=0.0, op0=ALU.mult, op1=ALU.add,
                                                           accum_out=den[:, i:i + 1])
                    t.then_inc(den_ready, 1)
                    dve.wait_ge(den_ready, h - 7)
                nc.vector.reciprocal(rden, den).then_inc(rden_ready, 1)
                dve.wait_ge(rden_ready, h + 1)
                for i, (a, b) in enumerate(parts):
                    t = nc.vector.tensor_scalar(prob[:, a:b], prob[:, a:b], rden[:, i:i + 1], None, ALU.mult)
                t.then_inc(normed, 1)

            def out_low(h):
                dve.wait_ge(o_hi, h + 1)
                at = h if isinstance(h, int) else None
                dst = actB[:, h, SEQ:2 * SEQ] if at is not None else actB[:, bass.ds(h, 1), SEQ:2 * SEQ]
                src = actB[:, h, 0:SEQ] if at is not None else actB[:, bass.ds(h, 1), 0:SEQ]
                nc.vector.tensor_tensor(dst, bank[6][:, 0:SEQ], src.bitcast(f32), ALU.subtract).then_inc(o_lo, 1)

            def merged_low(c):
                for b in range(2):
                    dve.wait_ge(mt_hi, 2 * c + b + 1)
                    kt = 4 * c + 2 * b
                    nc.vector.tensor_tensor(actA[:, bass.ds(kt, 2), SEQ:2 * SEQ],
                                            bank[4 + b][:, :].rearrange("p (j s) -> p j s", j=2),
                                            actA[:, bass.ds(kt, 2), 0:SEQ].bitcast(f32),
                                            ALU.subtract).then_inc(mt_lo, 1)

            def scaled_low(dst_src, kt, bank_half, gains, done):
                dst, src = dst_src
                nc.vector.scalar_tensor_tensor(out=dst, in0=bank_half, scalar=smalls_sb[:, gains + kt:gains + kt + 1],
                                               in1=src.bitcast(f32), op0=ALU.mult, op1=ALU.subtract)\
                    .then_inc(done, 1)

            def x2t_low(c, banks):
                for b in range(2):
                    dve.wait_ge(x2t_hi, 4 * c + 2 * b + 2)
                    for j in range(2):
                        kt = 4 * c + 2 * b + j
                        scaled_low((actB[:, kt, SEQ:2 * SEQ], actB[:, kt, 0:SEQ]), kt,
                                   banks[b][:, j * SEQ:(j + 1) * SEQ], S_GFFN, x2t_lo)

            dve.wait_ge(gains_in, 16)
            for u in range(UPR):
                for kt in (KU * u, KU * u + 1):
                    if u == 0:
                        dve.wait_ge(tile_high, kt + 1)
                        nc.vector.tensor_tensor(w_lo[:, 0, kt, :], raw[:, 0, kt * NB:(kt + 1) * NB],
                                                w_hi[:, 0, kt, :].bitcast(f32), ALU.subtract).then_inc(tile_split, 1)
                    dve.wait_ge(h_hi, kt + 1)
                    scaled_low((actA[:, kt, SEQ:2 * SEQ], actA[:, kt, 0:SEQ]), kt, xt[:, kt, :], S_GATT, h_lo)
                if u > 0:
                    low(0, u)

            def normalise(nth):
                pair = 2 * ((3 * (nth // 2) + nth % 2) % 2)
                dve.wait_ge(rs_ready, nth + 1)
                nc.vector.tensor_tensor(rs8x, rs8, xrs8, ALU.mult).then_inc(rs_scaled, 1)
                dve.wait_ge(rs_scaled, nth + 1)
                for r in range(RT):
                    t = nc.vector.tensor_tensor(
                        tmp[:, r, :].rearrange("p (j d) -> p j d", j=4),
                        bank[pair + r][:, :].rearrange("p (j d) -> p j d", j=4),
                        rs8x[:, 4 * r:4 * r + 4].rearrange("p (j a) -> p j a", a=1).broadcast_to([P, 4, HD]), ALU.mult)
                t.then_inc(qn_done, 1)

            dve.wait_ge(ident_in, 32)
            for g in range(GROUPS):
                for m in range(3):
                    R = 3 * g + m
                    for u in range(UPR):
                        low(R + 1, u)
                        slot = UPR * m + u
                        j, at = slot // 6, slot % 6
                        h = 4 * (g - 1) + j
                        if g == 0 and slot == 5:
                            dve.wait_ge(sums_x, 2)
                            nc.vector.tensor_scalar(xms, xss, 1.0 / DM, EPS, ALU.mult, ALU.add).then_inc(ms_x, 1)
                        if g == 0 and slot == 6:
                            dve.wait_ge(rs_x, 1)
                            for r in range(RT):
                                nc.vector.tensor_copy(xrs8[:, 4 * r:4 * r + 4], xrs[:, r:r + 1].broadcast_to([P, 4]))\
                                    .then_inc(rs_x8, 1)
                            dve.wait_ge(rs_x8, 2)
                        if R == 0 and u == UPR - 1:
                            normalise(0)
                        elif u == 0 and m > 0 and R != 1:
                            normalise(2 * g + m - 1)
                        if g > 0 and at == 1:
                            if g == 3:
                                dve.wait_ge(prep_ready, h + 1)
                            softmax_head(h, prep if g == 3 else mask, g == 3)
                        elif g > 0 and at == 5:
                            out_low(h)
                        if u == (UPR - 1 if R else UPR - 2) and m < 2:
                            dve.wait_ge(sq_ready, 2 * g + m + 1)
                            nc.vector.tensor_reduce(out=ss8, in_=tmp[:, :, :].rearrange("p r (j d) -> p (r j) d", j=4),
                                                    axis=AX.X, op=ALU.add).then_inc(ss_ready, 1)
                            dve.wait_ge(ss_ready, 2 * g + m + 1)
                            if m == 0:
                                t = nc.vector.tensor_scalar(ms8, ss8, HD * EPS, None, ALU.add)
                            else:
                                t = nc.vector.tensor_scalar(ms8, ss8, 1.0 / HD, EPS, ALU.mult, ALU.add)
                            t.then_inc(ms_ready, 1)
                        if g == 0 and slot == 10:
                            dve.wait_ge(wf_split, 1)
                            nc.vector.tensor_tensor(wf_k[:, :, 1, :], wf_raw, wf_k[:, :, 0, :].bitcast(f32),
                                                    ALU.subtract).then_inc(wf_split, 1)
                        if g == 0 and slot == 20:
                            dve.wait_ge(fa_rows, 1)
                            dve.wait_ge(smalls_in, 16)
                            for r in range(RT):
                                nc.vector.scalar_tensor_tensor(
                                    out=fz[:, 8 * r:8 * r + 8], in0=bank[5][:, 8 * r:8 * r + 8], scalar=xrs[:, r:r + 1],
                                    in1=smalls_sb[:, S_BF:S_BF + 8], op0=ALU.mult, op1=ALU.add).then_inc(fa_sum, 1)
                            dve.wait_ge(fa_sum, 2)
                            nc.vector.tensor_scalar(fb, fz, -1.0, None, ALU.mult).then_inc(fa_neg, 1)
                            dve.wait_ge(fa_neg, 1)
                            nc.vector.tensor_tensor(fn, fz, fb, ALU.min).then_inc(fa_arg, 1)
                        if g == 0 and slot == 21:
                            dve.wait_ge(fa_ln, 1)
                            nc.vector.scalar_tensor_tensor(out=lf_keep, in0=fz, scalar=0.0, in1=fn, op0=ALU.min,
                                                           op1=ALU.subtract).then_inc(lf_ready, 1)
                            dve.wait_ge(consts_in, 16)

            with dve.Fori(0, 4) as c:
                for m in range(2):
                    R = GATE0 + m + 2 * c
                    for u in range(UPR):
                        low(R + 1, u)
                        if m == 0 and u == 1:
                            softmax_head(12 + c, prep, True)
                        elif m == 0 and u == 7:
                            out_low(12 + c)

            def fox_part(c):
                dve.wait_ge(used, UPR * (BR0 + c) + 4)
                for r in range(RT):
                    t = nc.vector.tensor_tensor(tmp[:, r, :], bank[r][:, :], ga[:, r, bass.ds(c * NB, NB)], ALU.mult)
                t.then_inc(fox_merged, 1)

            def dil_part(c):
                dve.wait_ge(used, UPR * (BR0 + c) + UPR)
                for r in range(RT):
                    part = gb[:, r, bass.ds(c * NB, NB)]
                    t = nc.vector.tensor_tensor(part, bank[2 + r][:, :], part, ALU.mult)
                t.then_inc(dil_merged, 1)
                dve.wait_ge(dil_merged, c + 1)
                nc.vector.tensor_tensor(tmp[:, :, :], tmp[:, :, :], gb[:, :, bass.ds(c * NB, NB)], ALU.add)\
                    .then_inc(merged, 1)

            dve.wait_ge(act_evac, 4 + 8)
            for u in range(UPR):
                low(BR0 + 1, u)
                if u == 3:
                    fox_part(0)
            dil_part(0)
            with dve.Fori(1, 4) as c:
                for u in range(UPR):
                    low(BR0 + 1 + c, u)
                    if u == 3:
                        merged_low(c - 1)
                        dve.wait_ge(mt_ready, 2 * c)
                        fox_part(c)
                dil_part(c)

            for c in range(4):
                R = OUT0 + c
                for u in range(UPR):
                    low(R + 1, u)
                    if u == 3 and c == 0:
                        merged_low(3)
                    elif u == 3:
                        x2t_low(c - 1, bank[4:6])
                if c == 0:
                    dve.wait_ge(x_again, 16)
                dve.wait_ge(used, UPR * R + UPR)
                for r in range(RT):
                    part = xr[:, r, c * NB:(c + 1) * NB]
                    t = nc.vector.tensor_tensor(part, bank[2 * (c % 2) + r][:, :], part, ALU.add)
                t.then_inc(x2_done, 1)
                if c == 0:
                    nc.vector.memset(upad[:, :, 0:2], 0.0).then_inc(d_added, 1)

            def add_up(q, b0):
                dve.wait_ge(low_copied, q + 1)
                nc.vector.tensor_tensor(tmp_j, acc[:, b0:b0 + CT, 0:SEQ], tmp_j, ALU.add).then_inc(up_added, 1)
                dve.wait_ge(up_added, q + 1)
                nc.vector.tensor_tensor(upad[:, :, 2:2 + SEQ], tmp_j,
                                        rstd_row.rearrange("p (a s) -> p a s", a=1).broadcast_to([P, CT, SEQ]),
                                        ALU.mult).then_inc(u_ready, 1)

            def older_taps(q, ct):
                dve.wait_ge(tap2, q + 1)
                for tap, done in ((1, tap1), (0, conv_done)):
                    for j in range(CT):
                        t = nc.vector.scalar_tensor_tensor(
                            out=conv[:, j, :], in0=upad[:, j, tap:tap + SEQ],
                            scalar=smalls_sb[:, bass.ds(S_WC + 88 * tap + ct + j, 1)], in1=conv[:, j, :],
                            op0=ALU.mult, op1=ALU.add)
                    t.then_inc(done, 1)
                    dve.wait_ge(done, q + 1)

            def hidden(i):
                dve.wait_ge(silu_done, i + 1)
                nc.vector.tensor_tensor(tmp_j, conv, silu, ALU.mult).then_inc(a_ready, 1)

            def hidden_low(i, first_kt=0):
                dve.wait_ge(a_hi, i + 1)
                k = slice(first_kt, first_kt + CT)
                nc.vector.tensor_tensor(actA[:, k, SEQ:2 * SEQ], tmp_j, actA[:, k, 0:SEQ].bitcast(f32),
                                        ALU.subtract).then_inc(a_lo, 1)

            def add_down(R, c, first_bank=0, row0=None):
                if row0 is not None:
                    dve.wait_ge(row0, 1)
                else:
                    dve.wait_ge(used, UPR * R + 2 * c + 2)
                pair = (first_bank + 2 * c) % 8
                for r in range(RT):
                    if row0 is not None and r == 1:
                        dve.wait_ge(used, UPR * R + 2 * c + 2)
                    part = xr[:, r, c * NB:(c + 1) * NB]
                    nc.vector.tensor_tensor(part, bank[pair + r][:, :], part, ALU.add).then_inc(d_added, 1)

            for u in range(UPR):
                low(FF0 + 1, u)
                if u == 0:
                    dve.wait_ge(x2_sq, 8)
                    nc.vector.tensor_reduce(out=xss, in_=ssp.rearrange("p (r c) -> p r c", r=RT), axis=AX.X,
                                            op=ALU.add).then_inc(sums_x, 1)
                    dve.wait_ge(sums_x, 3)
                    nc.vector.tensor_scalar(xms, xss, 1.0 / DM, EPS, ALU.mult, ALU.add).then_inc(ms_x, 1)
                elif u == 2:
                    dve.wait_ge(rs_x, 2)
                    for r in range(RT):
                        t = nc.vector.tensor_scalar(diag[:, r * P:(r + 1) * P], ident, xrs2[:, r:r + 1], None, ALU.mult)
                    t.then_inc(diag_ready, 1)
                elif u == 3:
                    x2t_low(3, bank[0:2])
            dve.wait_ge(bc_done, 1)
            add_up(0, 4)

            def value_round(V, i):
                for u in range(UPR):
                    low(V + 1, u)
                    if u == 1:
                        older_taps(2 * i, 4 * i)
                add_up(2 * i + 1, 0)

            def gate_round(G, i):
                for u in range(UPR):
                    low(G + 1, u)
                    if u == 1:
                        older_taps(2 * i + 1, 44 + 4 * i)
                    elif u == 2:
                        hidden(i)
                    elif u == 3:
                        hidden_low(i)
                add_up(2 * i + 2, 4)

            with dve.Fori(0, BLOCKS - 2) as i:
                value_round(FF0 + 1 + 3 * i, i)
                gate_round(FF0 + 2 + 3 * i, i)
                for u in range(UPR):
                    low(FF0 + 4 + 3 * i, u)
                    if u % 2 == 1:
                        add_down(FF0 + 3 + 3 * i, u // 2)
            value_round(V_PREV, BLOCKS - 2)
            gate_round(G_LAST, BLOCKS - 2)
            value_round(V_LAST, BLOCKS - 1)
            for u in range(UPR):
                low(D_LAST, u)
                if u == 1:
                    older_taps(2 * BLOCKS - 1, 44 + 4 * (BLOCKS - 1))
                elif u == 2:
                    hidden(BLOCKS - 1)
                elif u == 3:
                    hidden_low(BLOCKS - 1, CT)
                if u % 2 == 1:
                    add_down(D_PREV, u // 2, 4)
            for c in range(4):
                add_down(D_LAST, c, 4, row0_done if c == 3 else None)

        @block.gpsimd
        def _(pool):
            def prepare_fox(h):
                if h:
                    pool.wait_ge(scores, h)
                for i, (mat, r) in enumerate(((upper, 0), (upper, 1), (ones, 0))):
                    t = nc.gpsimd.tensor_scalar(prep[:, i * P:(i + 1) * P], mat,
                                                lf_keep[:, 8 * r + h:8 * r + h + 1], None, ALU.mult)
                t.then_inc(prep_ready, 1)

            def prepare_dil(h):
                pool.wait_ge(row_max, h)
                nc.gpsimd.tensor_copy(slope, smalls_sb[:, bass.ds(S_SLOPE + h - 8, 1)]).then_inc(slope_now, 1)
                pool.wait_ge(slope_now, h - 7)
                return nc.gpsimd.tensor_tensor(prep[:, :], neg_dist, slope.broadcast_to([P, 3 * P]), ALU.mult)

            def prepare(h):
                if h < 8:
                    prepare_fox(h)
                elif h < 12:
                    prepare_dil(h).then_inc(prep_ready, 1)

            def head_rms(nth):
                pool.wait_ge(ms_ready, nth + 1)
                nc.gpsimd.tensor_tensor(rs8, ms8, mhalf, ALU.pow).then_inc(rs_ready, 1)

            nc.gpsimd.memset(actB[:, KT - 1, :].bitcast(f32), 0.0).then_inc(warm_data, 1)
            nc.gpsimd.memset(st[:, 91:92], 1.0).then_inc(warm, 1)
            nc.gpsimd.memset(wf[:, 16 * KT:].bitcast(f32), 0.0).then_inc(pad_done, 1)
            pool.wait_ge(ident_in, 32)
            pool.wait_ge(ms_x, 1)
            nc.gpsimd.tensor_tensor(xrs, xms, mhalf[:, 0:2], ALU.pow).then_inc(rs_x, 1)
            head_rms(0)
            head_rms(1)
            pool.wait_ge(lf_ready, 1)
            pool.wait_ge(consts_in, 16)
            prepare(0)
            for g in range(1, GROUPS):
                h = 4 * (g - 1)
                prepare(h + 1)
                head_rms(2 * g)
                prepare(h + 2)
                prepare(h + 3)
                head_rms(2 * g + 1)
                prepare(h + 4)
            pool.wait_ge(qkt_ready, 16)
            pool.wait_ge(qkt_done, 16)
            pool.wait_ge(act_evac, 4)
            with pool.Fori(0, 4) as c:
                pool.wait_ge(o_ready, 12 + c)
                nc.gpsimd.tensor_copy(q_now, q_of(3)[:, bass.ds(c, 1), :])
                nc.gpsimd.tensor_copy(v_now, v_of(3)[:, :, bass.ds(c * P, P)])
                prepare_dil(12 + c).then_inc(prep_ready, 1)
            pool.wait_ge(ms_x, 2)
            nc.gpsimd.tensor_tensor(xrs2, xms, mhalf[:, 0:2], ALU.pow).then_inc(rs_x, 1)


def _constants():
    c = np.zeros((P, C_N), np.float32)
    i, s = np.arange(P)[:, None], np.arange(P)[None, :]
    c[:, C_U:C_U + P] = i <= s
    c[:, C_M:C_M + P] = 1.0
    c[:, C_M + P:C_M + 2 * P] = i > s
    for n, d in enumerate((i - s, i - s + P, i - s)):
        at = slice(n * P, (n + 1) * P)
        n_patterns = ((d >= 0) & (d <= 128)) * 1 + ((d >= 0) & (d % 4 == 0)) * 1 + ((d >= 0) & (d % 16 == 0)) * 1
        c[:, C_MASK:C_MASK + 3 * P][:, at] = np.where(d >= 0, 0.0, NEG)
        c[:, C_ND:C_ND + 3 * P][:, at] = np.where(n_patterns > 0, -d, -1e34)
        c[:, C_CNT:C_CNT + 3 * P][:, at] = n_patterns
    return c


def kernel(x, g_attn, w_in, b_forget, g_q_fox, g_k_fox, g_q_dil, g_k_dil, w_br_fox, w_br_dil, w_out, g_ffn,
           w_up, w_conv, b_conv, w_down):
    import concourse.bacc as bacc
    from concourse.bass_utils import run_bass_kernel_spmd

    def tiles(v):
        return np.asarray(v).reshape(-1, P).T

    gq = [np.asarray(a)[0] for a in (g_q_fox, g_k_fox, g_q_dil, g_k_dil)]
    blocks = []
    for g in range(GROUPS):
        for m in range(2):
            blocks.append(gq[2 * (g // 2) + m][4 * (g % 2):4 * (g % 2) + 4].T)
    slopes = np.asarray(2.0 ** (-np.arange(1, 9)), np.float32)
    smalls = np.ascontiguousarray(np.concatenate(
        [np.eye(P, dtype=np.float32), tiles(np.asarray(g_attn)[0]), tiles(np.asarray(g_ffn)[0])] + blocks
        + [np.full((P, 8), -0.5, np.float32), (np.arange(P)[:, None] % 8 == np.arange(8)).astype(np.float32)]
        + [tiles(np.asarray(w_conv)[0, t]) for t in range(3)] + [tiles(np.asarray(b_conv)[0])]
        + [np.broadcast_to(np.asarray(b_forget)[0], (P, 8)), np.broadcast_to(slopes, (P, 8))], axis=1))
    assert smalls.shape == (P, S_N)
    x_t = np.ascontiguousarray(np.asarray(x)[0].T.reshape(KT, P, SEQ).transpose(1, 0, 2))
    arrays = {"x": np.asarray(x), "x_t": x_t, "smalls": smalls, "consts": _constants(), "w_in": np.asarray(w_in)[0],
              "w_fox": np.asarray(w_br_fox)[0], "w_dil": np.asarray(w_br_dil)[0], "w_out": np.asarray(w_out)[0],
              "w_up": np.asarray(w_up)[0], "w_down": np.asarray(w_down)[0]}
    nc = bacc.Bacc("TRN2", target_bir_lowering=False, num_devices=1)
    f32 = mybir.dt.float32
    aps = [nc.dram_tensor(n, a.shape, f32, kind="ExternalInput").ap() for n, a in arrays.items()]
    aps.append(nc.dram_tensor("out", (1, SEQ, DM), f32, kind="ExternalOutput").ap())
    decoder_layer(nc, *aps)
    r = run_bass_kernel_spmd(nc, [arrays], core_ids=[0])
    return r.results[0]["out"]
```
